# Optimizing a Trainium2 kernel written in Bass

```python
import jax, jax.numpy as jnp
from jax import lax
import numpy as np

D_MODEL = 1024
BATCH = 1
SEQ = 256
DEPTH = 1
DEC_BATCH = 8
DEC_SEQ = 4
PAST_LEN = 2048
PAGE_SIZE = 128

RW_HEADS = 8
RW_HEAD_DIM = 64
RW_WIDTH = RW_HEADS * RW_HEAD_DIM
DECAY_LORA = 64
ICLR_LORA = 64
GATE_LORA = 128
RW_PROJ = 3 * RW_WIDTH + DECAY_LORA + ICLR_LORA + GATE_LORA
GN_EPS = 64e-5
CONV_WIDTH = D_MODEL - RW_WIDTH
CONV_GROUPS = 8
CONV_K = 31
LN_EPS = 1e-5
MIX_WIDTH = RW_WIDTH + CONV_WIDTH
IN_PROJ = RW_PROJ + 2 * CONV_WIDTH
N_MEM = 256
X_HEADS = 4
X_HEAD_DIM = D_MODEL // X_HEADS
ATTN_SCALE = X_HEAD_DIM ** -0.5
N_EXPERTS = 32
TOP_K = 4
D_EXPERT = D_MODEL
SWIGLU_LIMIT = 7.0
SWIGLU_ALPHA = 1.702
NORM_EPS = 1e-5

kernel_name = "hybrid_rwkv7_conformer_memxattn_moe_step"

def rms_norm(x, g):
    xf = x.astype(jnp.float32)
    y = xf * lax.rsqrt(jnp.mean(xf * xf, axis=-1, keepdims=True) + NORM_EPS)
    return (y * g.astype(jnp.float32)).astype(x.dtype)

def _wkv7_step(S, inp):
    r_t, d_t, k_t, v_t, a_t, b_t = inp
    sa = jnp.einsum('bhij,bhj->bhi', S, a_t)
    S = S * d_t[:, :, None, :] + sa[..., None] * b_t[:, :, None, :] + v_t[..., None] * k_t[:, :, None, :]
    y = jnp.einsum('bhij,bhj->bhi', S, r_t)
    return S, y

def rwkv7_group(p, prev, s0, mu, w0, w_dup, a0, a_up, g_up, k_k, k_a, r_k, gn_g, gn_b):
    B, T, _ = p.shape
    H, N = RW_HEADS, RW_HEAD_DIM
    f32 = jnp.float32
    ps = jnp.concatenate([prev[:, None, :], p[:, :-1, :]], axis=1)
    z = p + mu * (ps - p)
    c1, c2, c3 = RW_WIDTH, 2 * RW_WIDTH, 3 * RW_WIDTH
    c4 = c3 + DECAY_LORA
    c5 = c4 + ICLR_LORA
    r, k, v = z[..., :c1], z[..., c1:c2], z[..., c2:c3]
    wd, ad, gd = z[..., c3:c4], z[..., c4:c5], z[..., c5:]
    w = -jax.nn.softplus(-(w0 + jnp.tanh(wd) @ w_dup)) - 0.5
    a = jax.nn.sigmoid(a0 + ad @ a_up)
    g = jax.nn.sigmoid(gd) @ g_up
    heads = lambda t: t.reshape(B, T, H, N).astype(f32)
    r, w, k, v, a = heads(r), heads(w), heads(k), heads(v), heads(a)
    kk = k * k_k.reshape(H, N).astype(f32)
    kk = kk / jnp.maximum(jnp.sqrt(jnp.sum(kk * kk, axis=-1, keepdims=True)), 1e-12)
    k = k * (1.0 + (a - 1.0) * k_a.reshape(H, N).astype(f32))
    decay = jnp.exp(-jnp.exp(w))
    xs = tuple(jnp.moveaxis(t, 1, 0) for t in (r, decay, k, v, -kk, kk * a))
    s_fin, y = lax.scan(_wkv7_step, s0.astype(f32), xs)
    y = jnp.moveaxis(y, 0, 1)
    mean = jnp.mean(y, axis=-1, keepdims=True)
    var = jnp.mean(jnp.square(y - mean), axis=-1, keepdims=True)
    yn = (y - mean) * lax.rsqrt(var + GN_EPS) * gn_g.reshape(H, N).astype(f32) + gn_b.reshape(H, N).astype(f32)
    bonus = jnp.sum(r * k * r_k.astype(f32), axis=-1, keepdims=True) * v
    out = ((yn + bonus).reshape(B, T, RW_WIDTH) * g.astype(f32)).astype(p.dtype)
    return out, p[:, -1, :], s_fin.astype(s0.dtype)

def conv_group(p, buf, dw_w, dw_b, ln_g, ln_b):
    u = p[..., :CONV_WIDTH] * jax.nn.sigmoid(p[..., CONV_WIDTH:])
    ext = jnp.concatenate([buf.astype(u.dtype), u], axis=1)
    c = lax.conv_general_dilated(ext, dw_w[:, None, :].astype(u.dtype), window_strides=(1,), padding='VALID',
                                 dimension_numbers=('NWC', 'WIO', 'NWC'),
                                 feature_group_count=CONV_WIDTH) + dw_b
    cf = c.astype(jnp.float32)
    mean = jnp.mean(cf, axis=-1, keepdims=True)
    var = jnp.mean(jnp.square(cf - mean), axis=-1, keepdims=True)
    cn = (cf - mean) * lax.rsqrt(var + LN_EPS) * ln_g.astype(jnp.float32) + ln_b.astype(jnp.float32)
    return jax.nn.silu(cn).astype(p.dtype), ext[:, -(CONV_K - 1):, :]

def memory_kv(mem, g_mem, w_mk, w_mv):
    B = mem.shape[0]
    m = rms_norm(mem, g_mem)
    k = (m @ w_mk).reshape(B, N_MEM, X_HEADS, X_HEAD_DIM)
    v = (m @ w_mv).reshape(B, N_MEM, X_HEADS, X_HEAD_DIM)
    return k, v

def cross_attn(h, mk, mv, w_q, w_o):
    B, T, _ = h.shape
    f32 = jnp.float32
    q = (h @ w_q).reshape(B, T, X_HEADS, X_HEAD_DIM)
    s = jnp.einsum('bthd,bmhd->bhtm', q.astype(f32), mk.astype(f32)) * ATTN_SCALE
    pr = jax.nn.softmax(s, axis=-1)
    o = jnp.einsum('bhtm,bmhd->bthd', pr, mv.astype(f32)).reshape(B, T, D_MODEL).astype(h.dtype)
    return o @ w_o

def moe(h, w_router, b_router, w_gate, b_gate, w_up, b_up, w_down, b_down):
    B, T, D = h.shape
    t = h.reshape(B * T, D)
    logits = (t @ w_router + b_router).astype(jnp.float32)
    top_v, top_i = lax.top_k(logits, TOP_K)
    probs = jax.nn.softmax(top_v, axis=-1)
    comb = jnp.sum(jax.nn.one_hot(top_i, N_EXPERTS, dtype=jnp.float32) * probs[..., None], axis=1)
    y = jnp.zeros((B * T, D), jnp.float32)
    for e in range(N_EXPERTS):
        gate = jnp.minimum(t @ w_gate[e] + b_gate[e], SWIGLU_LIMIT)
        up = jnp.clip(t @ w_up[e] + b_up[e], -SWIGLU_LIMIT, SWIGLU_LIMIT)
        hid = (up + 1.0) * gate * jax.nn.sigmoid(gate * SWIGLU_ALPHA)
        y = y + comb[:, e:e + 1] * (hid @ w_down[e] + b_down[e]).astype(jnp.float32)
    return y.astype(h.dtype).reshape(B, T, D)

def layer(x, mk, mv, prev, s0, buf, lw):
    h = rms_norm(x, lw['g_mix'])
    p = h @ lw['w_in']
    rw, new_prev, new_s = rwkv7_group(p[..., :RW_PROJ], prev, s0, lw['mu_shift'], lw['w0'], lw['w_decay_up'],
                                      lw['a0'], lw['w_iclr_up'], lw['w_glora_up'], lw['k_k'], lw['k_a'],
                                      lw['r_k'], lw['gn_g'], lw['gn_b'])
    cv, new_buf = conv_group(p[..., RW_PROJ:], buf, lw['dw_w'], lw['dw_b'], lw['cln_g'], lw['cln_b'])
    x = x + jnp.concatenate([rw, cv], axis=-1) @ lw['w_out']
    x = x + cross_attn(rms_norm(x, lw['g_xattn']), mk, mv, lw['w_q'], lw['w_o'])
    x = x + moe(rms_norm(x, lw['g_moe']), lw['w_router'], lw['b_router'], lw['w_moe_gate'], lw['b_moe_gate'],
                lw['w_moe_up'], lw['b_moe_up'], lw['w_moe_down'], lw['b_moe_down'])
    return x, new_prev, new_s, new_buf

def setup_inputs(seed: int = 0) -> dict:
    key = jax.random.key(seed)
    ks = iter(jax.random.split(key, 64))
    nrm = lambda shape, s: jax.random.normal(next(ks), shape, jnp.float32) * s
    L, D, E, F = DEPTH, D_MODEL, N_EXPERTS, D_EXPERT
    return {
        'x_prompt': nrm((BATCH, SEQ, D), 1.0),
        'x_sample': nrm((DEC_BATCH, DEC_SEQ, D), 1.0),
        'mem_prompt': nrm((BATCH, N_MEM, D), 1.0),
        'state_shift': nrm((L, DEC_BATCH, RW_PROJ), 1.0),
        'state_wkv': nrm((L, DEC_BATCH, RW_HEADS, RW_HEAD_DIM, RW_HEAD_DIM), 1.0),
        'state_conv': nrm((L, DEC_BATCH, CONV_K - 1, CONV_WIDTH), 0.5),
        'cache_mem_k': nrm((L, DEC_BATCH, N_MEM, X_HEADS, X_HEAD_DIM), 1.0),
        'cache_mem_v': nrm((L, DEC_BATCH, N_MEM, X_HEADS, X_HEAD_DIM), 1.0),
        'g_mix': 1.0 + nrm((L, D), 0.02),
        'w_in': nrm((L, D, IN_PROJ), D ** -0.5),
        'mu_shift': jax.random.uniform(next(ks), (L, RW_PROJ), jnp.float32, 0.0, 1.0),
        'w0': jax.random.uniform(next(ks), (L, RW_WIDTH), jnp.float32, -6.0, -0.5),
        'w_decay_up': nrm((L, DECAY_LORA, RW_WIDTH), 0.1),
        'a0': nrm((L, RW_WIDTH), 0.1),
        'w_iclr_up': nrm((L, ICLR_LORA, RW_WIDTH), 0.5 * ICLR_LORA ** -0.5),
        'w_glora_up': nrm((L, GATE_LORA, RW_WIDTH), GATE_LORA ** -0.5),
        'k_k': 0.85 + nrm((L, RW_WIDTH), 0.02),
        'k_a': 1.0 + nrm((L, RW_WIDTH), 0.02),
        'r_k': nrm((L, RW_HEADS, RW_HEAD_DIM), 0.1),
        'gn_g': 1.0 + nrm((L, RW_WIDTH), 0.02),
        'gn_b': nrm((L, RW_WIDTH), 0.01),
        'dw_w': nrm((L, CONV_K, CONV_WIDTH), CONV_K ** -0.5),
        'dw_b': nrm((L, CONV_WIDTH), 0.01),
        'cln_g': 1.0 + nrm((L, CONV_WIDTH), 0.02),
        'cln_b': nrm((L, CONV_WIDTH), 0.01),
        'w_out': nrm((L, MIX_WIDTH, D), MIX_WIDTH ** -0.5),
        'g_xattn': 1.0 + nrm((L, D), 0.02),
        'g_mem': 1.0 + nrm((L, D), 0.02),
        'w_q': nrm((L, D, D), D ** -0.5),
        'w_mk': nrm((L, D, D), D ** -0.5),
        'w_mv': nrm((L, D, D), D ** -0.5),
        'w_o': nrm((L, D, D), D ** -0.5),
        'g_moe': 1.0 + nrm((L, D), 0.02),
        'w_router': nrm((L, D, E), D ** -0.5),
        'b_router': nrm((L, E), 0.01),
        'w_moe_gate': nrm((L, E, D, F), D ** -0.5),
        'b_moe_gate': nrm((L, E, F), 0.01),
        'w_moe_up': nrm((L, E, D, F), D ** -0.5),
        'b_moe_up': nrm((L, E, F), 0.01),
        'w_moe_down': nrm((L, E, F, D), F ** -0.5),
        'b_moe_down': nrm((L, E, D), 0.01),
        'g_final': 1.0 + nrm((D,), 0.02),
    }

def reference(x_prompt, x_sample, mem_prompt, state_shift, state_wkv, state_conv, cache_mem_k, cache_mem_v,
              g_mix, w_in, mu_shift, w0, w_decay_up, a0, w_iclr_up, w_glora_up, k_k, k_a, r_k, gn_g, gn_b,
              dw_w, dw_b, cln_g, cln_b, w_out, g_xattn, g_mem, w_q, w_mk, w_mv, w_o,
              g_moe, w_router, b_router, w_moe_gate, b_moe_gate, w_moe_up, b_moe_up, w_moe_down, b_moe_down,
              g_final):
    bp = x_prompt.shape[0]
    dt = x_prompt.dtype
    xp, xs = x_prompt, x_sample
    sh_p_l, wkv_p_l, cv_p_l, mk_p_l, mv_p_l = [], [], [], [], []
    sh_s_l, wkv_s_l, cv_s_l = [], [], []
    for l in range(DEPTH):
        lw = dict(g_mix=g_mix[l], w_in=w_in[l], mu_shift=mu_shift[l], w0=w0[l], w_decay_up=w_decay_up[l],
                  a0=a0[l], w_iclr_up=w_iclr_up[l], w_glora_up=w_glora_up[l], k_k=k_k[l], k_a=k_a[l],
                  r_k=r_k[l], gn_g=gn_g[l], gn_b=gn_b[l], dw_w=dw_w[l], dw_b=dw_b[l], cln_g=cln_g[l],
                  cln_b=cln_b[l], w_out=w_out[l], g_xattn=g_xattn[l], w_q=w_q[l], w_o=w_o[l],
                  g_moe=g_moe[l], w_router=w_router[l], b_router=b_router[l], w_moe_gate=w_moe_gate[l],
                  b_moe_gate=b_moe_gate[l], w_moe_up=w_moe_up[l], b_moe_up=b_moe_up[l],
                  w_moe_down=w_moe_down[l], b_moe_down=b_moe_down[l])
        mk_p, mv_p = memory_kv(mem_prompt, g_mem[l], w_mk[l], w_mv[l])
        prev0 = jnp.zeros((bp, RW_PROJ), dt)
        s00 = jnp.zeros((bp, RW_HEADS, RW_HEAD_DIM, RW_HEAD_DIM), dt)
        buf0 = jnp.zeros((bp, CONV_K - 1, CONV_WIDTH), dt)
        xp, sh_p, wkv_p, cv_p = layer(xp, mk_p, mv_p, prev0, s00, buf0, lw)
        xs, sh_s, wkv_s, cv_s = layer(xs, cache_mem_k[l], cache_mem_v[l], state_shift[l], state_wkv[l],
                                      state_conv[l], lw)
        sh_p_l.append(sh_p); wkv_p_l.append(wkv_p); cv_p_l.append(cv_p)
        mk_p_l.append(mk_p); mv_p_l.append(mv_p)
        sh_s_l.append(sh_s); wkv_s_l.append(wkv_s); cv_s_l.append(cv_s)
    y_prompt = rms_norm(xp, g_final)
    y_sample = rms_norm(xs, g_final)
    return (y_prompt, y_sample,
            jnp.stack(sh_p_l), jnp.stack(wkv_p_l), jnp.stack(cv_p_l), jnp.stack(mk_p_l), jnp.stack(mv_p_l),
            jnp.stack(sh_s_l), jnp.stack(wkv_s_l), jnp.stack(cv_s_l))


_drawn_inputs = setup_inputs


def setup_inputs(seed=0):
    import zlib

    import numpy as np

    out = dict(_drawn_inputs(seed))
    spreads = {}
    factors = {'k_k': 8.415,
     'gn_b': 8.0,
     'dw_b': 2.865,
     'g_mem': 3.112,
     'b_moe_gate': 8.0,
     'b_moe_up': 8.0,
     'b_moe_down': 8.0,
     'g_final': 8.241,
     'k_a': 2.718,
     'gn_g': 3.227,
     'cln_b': 3.576}
    for name, (base, spread) in spreads.items():
        noise = np.random.default_rng([zlib.crc32(name.encode()), seed]).standard_normal(out[name].shape)
        drawn = base * np.exp(spread * noise) if base else spread * noise
        out[name] = __import__('jax').numpy.asarray(drawn.astype(out[name].dtype))
    for name, factor in factors.items():
        out[name] = (out[name] * factor).astype(out[name].dtype)
    return out
```

```python
from contextlib import ExitStack

import concourse.bass as bass
from concourse import mybir

F32 = mybir.dt.float32
I32 = mybir.dt.int32
ALU = mybir.AluOpType
ACT = mybir.ActivationFunctionType
AX = mybir.AxisListType

P = 128
D = 1024
KT = D // P
SEQ = 256
NB, NT = 8, 4
TOK = SEQ + NB * NT
TT = 3
NE, TOPK = 32, 4
CAP = 64
ROUNDS = -(-TOK // CAP)
PAIRS = NE // 2
SLOTS = 6
RW = 14
CT = 4
TAPS = 31
PEXT = 1 + SEQ + NB * (1 + NT)
EXT = TAPS - 1 + SEQ + NB * (TAPS - 1 + NT)
CH = 64
NC = 5
TW = NC * CH
MEM = 256
XH = 4
KAPPA = 0.6065306597126334
LEVELS = (2, 4, 8, 16, 32)
W_IN_ORDER = (12, 13, 4, 5, 6, 7, 0, 1, 2, 3, 8, 9, 10, 11, 14, 18, 15, 19, 16, 20, 17, 21)
VEC = dict(g_mix=0, g_mem=8, g_x=16, g_moe=24, mu=32, w0=46, a0=50, k_k=54, k_a=58, r_k=62, gn_g=66, gn_b=70,
           dw_b=74, cln_g=78, cln_b=82, dw_w=86)
VECW = 86 + CT * TAPS
CONST = dict(ident=(0, 128), ones=(128, 128), before=(256, 128), mean64=(384, 128), iota=(512, 64), istack=(576, 64),
             causal=(640, 128), causal_s=(768, 128), levels=(896, 6 * 64), of_sample=(1280, 8), not_sample=(1288, 8),
             valid=(1296, 3))
CONSTW = 1300
FRONT = ([("w_in", n, n % 2) for n in range(6)] + [("w_mk", n, n) for n in range(2)] + [("w_mv", n, n) for n in range(2)]
         + [("w_out", n, n) for n in range(2)] + [("w_q", n, 2 + n) for n in range(2)]
         + [("cache_k", n, (4 + n) % 6) for n in range(4)] + [("cache_v", n, 2 + n) for n in range(4)]
         + [("w_o", n, n) for n in range(2)])
FIRST_SLOT = 2
FRONT_FILLS = [sum(f[2] == i for f in FRONT) for i in range(SLOTS)]


def front_fill(name, part):
    at = [f[:2] for f in FRONT].index((name, part))
    slot = FRONT[at][2]
    return slot, sum(f[2] == slot for f in FRONT[:at])

def build(nc, A, O):
    with ExitStack() as ctx:
        def sb(name, shape, dt=F32):
            return ctx.enter_context(nc.sbuf_tensor(name, shape, dt))

        def sem(name):
            return ctx.enter_context(nc.semaphore(name))

        def part(base, at, *dims):
            n = 1
            for d in dims:
                n *= d
            a = base[:, at:at + n]
            names = "abcd"[:len(dims)]
            if len(dims) == 1:
                return a
            return a.rearrange(f"p ({' '.join(names)}) -> p {' '.join(names)}", **dict(zip(names, dims)))

        SLOT = 4 * D
        ring = sb("ring", [P, SLOTS * SLOT])
        scratch = ring[:, 2 * SLOT:]
        arena = sb("arena", [P, 23224])
        xT = sb("xT", [P, KT, TT * P])
        const = sb("const", [P, CONSTW])
        vec = sb("vec", [P, VECW])
        slot = [part(ring, i * SLOT, KT, 512) for i in range(SLOTS)]

        def C(name):
            at, n = CONST[name]
            return const[:, at:at + n]

        def V(name, c=0):
            return vec[:, VEC[name] + c:VEC[name] + c + 1]

        ident, ones, mean64, istack = C("ident"), C("ones"), C("mean64"), C("istack")

        eps = sb("eps", [P, 2])
        rs = sb("rs", [P, TOK])
        PC = sb("PC", [P, CT, NC - 1])
        PCs = sb("PCs", [P, CT, NB])
        shift_out = sb("shift_out", [P, RW, 1 + NB])
        amax = sb("amax", [P, 9])
        asum = sb("asum", [P, 9])
        hT = part(arena, 0, KT, TOK)
        memT = part(arena, 2304, KT, MEM)
        QB = part(arena, 0, NC, CT, 3 * CH)
        memK = part(arena, 4352, KT, MEM)
        memV = part(arena, 6400, 2, D)
        mix = part(arena, 8448, KT, TOK)
        ext = part(arena, 10752, CT, EXT)
        S0s = part(arena, 10752, CT, NB, CH)
        kk = part(arena, 12984, CT, TW)
        kmod = part(arena, 14264, CT, TW)
        tmp = part(arena, 15544, CT, TW)
        tmp2 = part(arena, 16824, CT, TW)
        QK = part(arena, 12984, NC, CT, 3 * CH)
        Vtok = part(arena, 16824, NC, CT, CH)
        gate = part(arena, 18104, CT, TW)
        QR = part(arena, 19384, CT, NC, 3 * CH)
        lora_wa = part(arena, 19384, 512)
        lora_g = part(arena, 19384 + 512, 512)
        shift_in = part(arena, 19384 + 1024, RW, NB)
        tlora = part(arena, 19384 + 1152, 2, TW)
        q = part(arena, 19384, KT, TOK)
        probs = part(arena, 12984, 8, MEM)
        probsT = part(arena, 15032, 2, 8, P)
        osam = part(arena, 17080, MEM)
        ssam = part(arena, 10752, NB, MEM)
        ssamT = part(arena, 2304, 2 * NB, P)
        rs_mem = tmp2[:, 0, 0:MEM]
        x_tok = part(arena, 0, TT, D)
        h_tok = part(arena, 3072, TT, D)
        g_row = arena[:, 6144:7168]
        gf_row = arena[:, 7168:8192]
        xe = part(arena, 8448, KT, 2, CAP)
        gmin = arena[:, 9472:9984]
        sig = arena[:, 9984:10496]
        b_gate = arena[0:NE, 10752:11776]
        b_up = arena[0:NE, 11776:12800]
        b_down = arena[0:NE, 12800:13824]
        ug = arena[:, 14336:14848]
        hid = arena[:, 14848:15360]
        hexT = part(arena, 15360, 4, 2, CAP)
        ye = arena[:, 15872:16384]
        gT = part(arena, 16384, 2, TT * P)
        pick = part(arena, 17152, TT, 2, CAP)
        wpick = part(arena, 17536, TT, 2, 2, CAP)
        combT = arena[0:NE, 18304:18688]
        one_e = part(arena, 18688, 2, CAP)[0:NE]
        w_r = part(arena, 18816, KT, NE)
        b_r = arena[:, 19072:19104]
        logit = part(arena, 19104, TT, NE)
        top8 = part(arena, 19200, TT, 8)
        over = part(arena, 19224, TT, NE)
        tie = part(arena, 19320, TT, NE)
        tiecum = part(arena, 19416, TT, NE)
        mask = part(arena, 19512, TT, NE)
        comb = part(arena, 19608, TT, NE + 2)
        pos = part(arena, 19710, TT, NE + 2)
        zero = arena[:, 19812:19844]
        need = arena[:, 19844:19847]
        esum = arena[:, 19847:19850]
        ntop = arena[:, 19850:19853]
        ssq = arena[:, 19853:19856]
        rstd = ssq
        load = arena[:, 19856:19857]
        load_i = sb("load_i", [P, 1], I32)
        y = x_tok
        before, iota, valid = C("before"), C("iota"), C("valid")
        pext = part(scratch, 0, RW, PEXT)
        z = part(scratch, 4160, RW, TW)
        sw = part(scratch, 8640, CT, TW)
        cum = part(scratch, 9920, CT, TW)
        Pm = part(scratch, 11200, CT, TW)
        Pinv = part(scratch, 12480, CT, TW)
        Pex = part(scratch, 13760, CT, TW)
        rmask = Pex
        iclr = part(scratch, 15040, CT, TW)
        bt = part(scratch, 0, CT, TW)
        kt = part(scratch, 1280, CT, TW)
        QS = part(scratch, 0, CT, CH)
        LT = part(scratch, 2560, NC, CT, P)
        X = part(scratch, 5120, NC, CT, P)
        XT = part(scratch, 7680, NC, CT, P)
        Zs = part(scratch, 10240, NC, CT, P)
        Mk = part(scratch, 12800, 2, CT, P)
        yT = part(scratch, 13824, CT, TW)
        Wsb = part(scratch, 15104, CT, CH)
        Usb = part(scratch, 15360, CT, CH)
        Ssb = part(scratch, 15616, CT, CH)
        S0T = part(scratch, 15872, CT, CH)
        WY = part(scratch, 16128, CT, CH)
        Um = part(scratch, 2560, CT, NB, CH)
        Vm = part(scratch, 4608, CT, NB, CH)
        Wf = part(scratch, 10240, CT, NB, CH)
        t1 = part(scratch, 10240, CT, TW)
        t2 = part(scratch, 11520, CT, TW)

        ps = ctx.enter_context(nc.psum_tensor("ps", [P, 8, 512], F32))

        psX = ps[:, 0:2, :].rearrange("p b f -> p (b f)")
        psY = ps[:, 2:4, :].rearrange("p b f -> p (b f)")
        psG, psU, psD, psT = (ps[:, b, :] for b in (4, 5, 6, 7))
        psP = [psX, psY]

        NAMES = """sum_ps x_in const_in mem_in lora_in shift_ld ext_ld state_ld sq_done root h_done mem_h
            pool_i p_ps p_out z_done convgate u_done tl lora_ps sw_done a_done g_done kk_done scan cumex exps pc_done
            mk_ps mk_out mv_ps mv_out prep mix_b v_ps v_out cm_ps cm_out tok_ps tok_out lt_copied x0t x0_ps x0_out
            m_ready z_ps z_out xz_ps x_add xt_ps xt_out ws_ps ws_out u_ps u_out ys_ps s_out y_out st_ps s0_out
            sf_ps wf um_ready sd_ps snew yc cm1 cc cnorm csig mix_done
            conv wout_ps xres q_ps q_out s_ps s_max s_exp s_norm pt_ps pt_out o_ps o_out
            sk_ps ss_max ss_exp ss_norm st2_ps st2_out sv_ps so_out so_ps oT_out wo_ps xres2 osent conv_sent state_sent dve_c
            small_in xt_done xt_out2 ssq_done xg_done logit_ps max_done exp_done mask_done pos_ps
            comb_done combT_ps combT_out ydown_ps route_ready h_ready
            pick_ready disp_done xe_ready one_ready gate_done g_ready sig_ready up_done wpickT_done gT_ready hid_ready hT_done hT_ready
            ye_ready scat_done y_added fin_ssq out_ready out_sent round_pos fin_recip pool_c dve_m""".split()
        S = {n: sem(n) for n in NAMES}
        slot_in = [sem(f"slot_in{i}") for i in range(SLOTS)]
        slot_free = [sem(f"slot_free{i}") for i in range(SLOTS)]
        block = ctx.enter_context(nc.Block())

        def counted(eng):
            n = {}

            def tell(name, ins, wait=True):
                ins.then_inc(S[name], 1)
                n[name] = n.get(name, 0) + 1
                if wait:
                    eng.wait_ge(S[name], n[name])
            return tell

        class Chain:
            def __init__(self, eng, s, base=0):
                self.eng, self.s, self.base, self.n = eng, s, base, 0

            def __call__(self, ins):
                ins.then_inc(self.s, 1)
                self.n += 1
                self.eng.wait_ge(self.s, self.base + self.n)

        @block.sync
        def _(sp):
            sp.dma_start(xT[:, :, :], A["xT"]).then_inc(S["x_in"], 16)
            sp.dma_start(const[:, :], A["const"]).then_inc(S["const_in"], 16)
            sp.dma_start(vec[:, :], A["vec"]).then_inc(S["const_in"], 16)
            sp.dma_start(memT, A["memT"]).then_inc(S["mem_in"], 16)

            sp.dma_start(shift_in, A["shift"]).then_inc(S["shift_ld"], 16)

            def fill(name, n, *waits):
                i, _ = front_fill(name, n)
                for s, v in waits:
                    sp.wait_ge(S[s], v)
                src = A[name][n]
                dst = part(ring, i * SLOT, src.shape[1])
                sp.dma_start(dst, src).then_inc(slot_in[i], 16)

            fill("w_in", 0)
            fill("w_in", 1)
            sp.dma_start(lora_wa, A["lora_wa"]).then_inc(S["lora_in"], 16)
            sp.dma_start(lora_g, A["lora_g"]).then_inc(S["lora_in"], 16)
            for c in range(CT):
                sp.dma_start(ext[:, c, TAPS - 1 + SEQ:].rearrange("p (b t) -> p b t", b=NB)[:, :, 0:TAPS - 1],
                             A["conv"][:, c, :, :]).then_inc(S["ext_ld"], 16)
            for n in range(2, 6):
                fill("w_in", n, ("p_ps", 4 * (n - 1)))
            fill("w_mk", 0, ("p_ps", 20))
            fill("w_mk", 1, ("p_ps", 22))
            fill("w_mv", 0, ("mk_ps", 4))
            fill("w_mv", 1, ("mk_ps", 8))
            fill("w_out", 0, ("mv_ps", 2))
            fill("w_out", 1, ("mv_ps", 4))
            sp.wait_ge(S["cm1"], 1)
            sp.wait_ge(S["conv_sent"], 16 * 9)
            sp.dma_start(S0s, A["states"]).then_inc(S["state_ld"], 16)
            fill("w_q", 0, ("mix_done", 1))
            fill("w_q", 1)
            fill("cache_k", 0)
            sp.wait_ge(S["state_sent"], 16)
            fill("cache_k", 1)
            fill("cache_k", 2, ("wout_ps", 4))
            fill("cache_k", 3, ("wout_ps", 8))
            fill("cache_v", 0, ("q_ps", 4))
            fill("cache_v", 1, ("q_ps", 8))
            fill("cache_v", 2, ("sk_ps", 1))
            fill("cache_v", 3, ("sk_ps", 2))
            fill("w_o", 0, ("sk_ps", 3))
            fill("w_o", 1, ("sk_ps", 4))
            sp.wait_ge(S["oT_out"], 1)
            sp.wait_ge(S["o_out"], 1)
            for dst, name in ((g_row, "g_moe_row"), (gf_row, "g_final_row"), (b_r, "b_router")):
                sp.dma_start(dst, A[name].broadcast_to([P, dst.shape[1]])).then_inc(S["small_in"], 16)
            for dst, name in ((w_r, "w_router"), (b_gate, "b_gate"), (b_up, "b_up"), (b_down, "b_down")):
                sp.dma_start(dst, A[name]).then_inc(S["small_in"], 16)
            MATRICES = ((A["w_gate"], 0), (A["w_up"], 0), (A["w_gate"], 1), (A["w_down"], 0), (A["w_up"], 1), (A["w_down"], 1))
            last_front = [("wo_ps", 4), ("wo_ps", 8)] + [("sv_ps", n + 1) for n in range(4)]

            def experts(q, s, first):
                for n, (w, p) in enumerate(MATRICES):
                    for c in range(2):
                        i = (FIRST_SLOT + 2 * n + c) % SLOTS
                        if first and n < 3:
                            sem_, val = last_front[i]
                            sp.wait_ge(S[sem_], val)
                        else:
                            sp.wait_ge(slot_free[i], 2 * s + n // 3)
                        src = w[bass.ds(2 * q + p, 1), c * 512:(c + 1) * 512, :]
                        sp.dma_start(part(ring, i * SLOT, 4, D), src.rearrange("a (k p) f -> p (a k) f", p=P)).then_inc(slot_in[i], 16)

            experts(0, 0, True)
            with sp.Fori(1, PAIRS) as q:
                experts(q, q, False)
            sp.wait_ge(S["route_ready"], 1)
            n = sp.value_load(load_i[0:1, 0:1], min_val=0, max_val=TOK)
            with sp.Fori(1, ROUNDS) as r:
                with sp.If(n > r * CAP):
                    with sp.Fori(0, PAIRS) as q:
                        experts(q, r * PAIRS + q, False)
            for j in range(TT):
                sp.wait_ge(S["out_ready"], j + 1)
                sp.dma_start(O["y"][:, j, :], h_tok[:, j, :]).then_inc(S["out_sent"], 16)
            sp.wait_ge(S["out_sent"], 16 * TT)
            sp.wait_ge(S["osent"], 16 * 3)
            sp.wait_ge(S["conv_sent"], 16 * 9)
            sp.wait_ge(S["state_sent"], 16)

        def rounds(eng, n, step_fn, before_round=None):
            with eng.Fori(0, ROUNDS) as r:
                with eng.If(n > r * CAP):
                    if before_round:
                        before_round(r)
                    with eng.Fori(0, PAIRS) as q:
                        step_fn(r, q, r * PAIRS + q)

        @block.gpsimd
        def _(pool):
            g = nc.gpsimd
            tell = counted(pool)
            tell("pool_i", g.memset(eps[:, 0:1], 1e-5), False)
            tell("pool_i", g.memset(eps[:, 1:2], 64e-5), False)
            tell("pool_i", g.memset(pext[:, :, 0:1], 0.0), False)
            tell("pool_i", g.memset(z[:, :, TOK:TW], 0.0), False)
            tell("pool_i", g.memset(ext[:, :, 0:TAPS - 1], 0.0), False)
            tell("pool_i", g.memset(rmask, 1.0))
            tell("pool_i", g.memset(rmask[:, :, 0:SEQ].rearrange("p c (n t) -> p c n t", t=CH)[:, :, :, 0:1], 0.0), False)
            tell("pool_i", g.memset(rmask[:, :, SEQ:TW].rearrange("p c (n t) -> p c n t", t=NT)[:, :, :, 0:1], 0.0), False)
            pool.wait_ge(S["shift_ld"], 16)
            tell("pool_i", g.tensor_copy(pext[:, :, 1 + SEQ:].rearrange("p c (b t) -> p c b t", b=NB)[:, :, :, 0:1],
                                         shift_in.unsqueeze(3)))

            pool.wait_ge(S["p_out"], 2 * RW)
            tell("pool_i", g.tensor_copy(shift_out[:, :, 0:1], pext[:, :, SEQ:SEQ + 1]), False)
            tell("pool_i", g.tensor_copy(shift_out[:, :, 1:].unsqueeze(3),
                                         pext[:, :, 1 + SEQ:].rearrange("p c (b t) -> p c b t", b=NB)[:, :, :, NT:NT + 1]))
            pool.dma_start(O["shift"], shift_out[:, :, :]).then_inc(S["conv_sent"], 16)
            pool.wait_ge(S["exps"], 1)
            tell("pc_done", g.tensor_copy(PC[:, :, :].unsqueeze(3),
                                          Pm.rearrange("p c (n t) -> p c n t", t=CH)[:, :, 0:NC - 1, CH - 1:CH]), False)
            tell("pc_done", g.tensor_copy(PCs[:, :, :].unsqueeze(3),
                                          Pm[:, :, SEQ:TOK].rearrange("p c (n t) -> p c n t", t=NT)[:, :, :, NT - 1:NT]))
            pool.wait_ge(S["u_done"], 2 * CT)
            for c in range(CT):
                pool.dma_start(O["conv"][:, c, 0, :], ext[:, c, SEQ:SEQ + TAPS - 1]).then_inc(S["conv_sent"], 16)
                pool.dma_start(O["conv"][:, c, 1:, :],
                               ext[:, c, TAPS - 1 + SEQ:].rearrange("p (b t) -> p b t", b=NB)[:, :, NT:]).then_inc(S["conv_sent"], 16)
            pool.wait_ge(S["prep"], 1)
            tell("lt_copied", g.tensor_copy(QR.rearrange("p c n t -> p (c n) t")[:, :, 2 * CH:],
                                            istack.unsqueeze(1).broadcast_to([P, CT * NC, CH])), False)
            pool.wait_ge(S["v_out"], 1)
            tell("lt_copied", g.memset(LT, 0.0))
            tell("lt_copied", g.memset(S0T, 0.0))
            for n in range(NC):
                pool.wait_ge(S["cm_out"], 2 * n + 1)
                for h in range(2):
                    o = slice(CH * h, CH * h + CH)
                    tell("lt_copied", g.tensor_copy(LT[o, n, :, o], QB[o, n, :, 0:CH]))
            pool.wait_ge(S["tok_ps"], NC)
            tell("lt_copied", g.tensor_copy(QS.rearrange("p c (a t) -> p c a t", a=2),
                                            QR[:, :, NC - 1, 0:2 * CH].rearrange("p c (a t) -> p c a t", a=2)[:, :, :, 0:NB * NT]))
            pool.wait_ge(S["mk_out"], 8)
            pool.dma_start(O["mem_k"], memK).then_inc(S["osent"], 16)
            pool.wait_ge(S["mv_out"], 4)
            pool.dma_start(O["mem_v"], memV).then_inc(S["osent"], 16)
            pool.wait_ge(S["s0_out"], NC - 1)
            pool.dma_start(O["state_p"], S0T).then_inc(S["state_sent"], 16)
            pool.wait_ge(S["snew"], 2)
            pool.dma_start(O["state_s"], S0s).then_inc(S["osent"], 16)
            pool.wait_ge(S["xres2"], KT)
            g.memset(zero, 1.0)
            g.memset(pos[:, :, NE:NE + 2], -1.0)
            tell("pool_c", g.memset(comb[:, :, NE:NE + 2], 0.0), False)
    
        @block.tensor
        def _(pe):
            readers = {}

            def take(*banks):
                for b in banks:
                    for s, v in readers.pop(b, []):
                        pe.wait_ge(S[s], v)

            def mm(out, lhsT, rhs, start=True, stop=True):
                return nc.tensor.matmul(out, lhsT, rhs, start=start, stop=stop)

            def linear(name, n, src, width, banks, done, first, reader, tiles=4):
                i, f = front_fill(name, n)
                pe.wait_ge(slot_in[i], 16 * (f + 1))
                for m in range(tiles):
                    b = banks[(first + m) % len(banks)]
                    take(b)
                    w = part(ring, i * SLOT, KT, 128 * tiles)
                    for k in range(KT):
                        last = mm(ps[:, b, 0:width], w[:, k, m * P:(m + 1) * P], src[:, k, 0:width], k == 0, k == KT - 1)
                    last.then_inc(S[done], 1)
                    readers[b] = [reader(first + m)]

            pe.wait_ge(S["const_in"], 32)
            for n, (src, w) in enumerate(((mix, TOK), (part(arena, 4352, KT, MEM), MEM))):
                pe.wait_ge(S["sq_done"], n + 1)
                for k in range(KT):
                    last = mm(ps[:, n, 0:w], ones, src[:, k, :], k == 0, k == KT - 1)
                last.then_inc(S["sum_ps"], 1)
                readers[n] = [("root", n + 1)]
            pe.wait_ge(S["h_done"], KT)

            def p_reader(i):
                c = W_IN_ORDER[i]
                if c < RW:
                    return "p_out", 2 * (i + 1)
                return "u_done", 2 * ((i - RW) // 2 + 1)

            for n in range(6):
                linear("w_in", n, hT, TOK, range(8), "p_ps", 4 * n, p_reader, 4 if n < 5 else 2)
            pe.wait_ge(S["lora_in"], 32)
            pe.wait_ge(S["tl"], 2)
            for c in range(CT):
                take(c)
                mm(ps[:, c, 0:TW], lora_wa[0:64, c * P:(c + 1) * P], tlora[0:64, 0, :]).then_inc(S["lora_ps"], 1)
            for c in range(CT):
                take(4 + c)
                mm(ps[:, 4 + c, 0:TW], lora_wa[64:P, c * P:(c + 1) * P], z[64:P, 12, :]).then_inc(S["lora_ps"], 1)
            for c in range(CT):
                pe.wait_ge(S["sw_done"], c + 1)
                mm(ps[:, c, 0:TW], lora_g[:, c * P:(c + 1) * P], tlora[:, 1, :]).then_inc(S["lora_ps"], 1)
                readers[c] = [("g_done", c + 1)]
                readers[4 + c] = [("a_done", c + 1)]
            pe.wait_ge(S["sq_done"], 3)
            for c in range(CT):
                take(4 + c)
                last = mm(ps[:, 4 + c, 0:TW], mean64, tmp[:, c, :])
                readers[4 + c] = [("root", 3)]
            last.then_inc(S["sum_ps"], 1)
            pe.wait_ge(S["mem_h"], KT)
            for n in range(2):
                linear("w_mk", n, memT, MEM, range(4), "mk_ps", 4 * n, lambda m: ("mk_out", m + 1))
            pe.wait_ge(S["prep"], 1)
            take(4, 5, 6, 7)
            for c in range(CT):
                last = mm(ps[:, 4 + c, 0:TW], mean64, tmp[:, c, :])
                readers[4 + c] = [("mix_b", 1)]
            last.then_inc(S["sum_ps"], 1)
            for n in range(2):
                i, f = front_fill("w_mv", n)
                pe.wait_ge(slot_in[i], 16 * (f + 1))
                for t in range(2):
                    b = 2 * n + t
                    take(b)
                    for k in range(KT):
                        last = mm(ps[:, b, :], memT[:, k, t * P:(t + 1) * P], slot[i][:, k, :], k == 0, k == KT - 1)
                    last.then_inc(S["mv_ps"], 1)
                    readers[b] = [("mv_out", b + 1)]
            H = [slice(0, CH), slice(CH, P)]
            take(4, 5, 6)
            for n in range(NC):
                for c in range(CT):
                    for o in H:
                        last = mm(ps[o, 4 + n // 2, (n % 2) * 256 + c * CH:(n % 2) * 256 + (c + 1) * CH],
                                  z[o, 8 + c, n * CH:(n + 1) * CH], ident[o, o])
            last.then_inc(S["v_ps"], 1)
            for b in (4, 5, 6):
                readers[b] = [("v_out", 1)]
            pe.wait_ge(S["lt_copied"], 1)
            for n in range(NC):
                for w, src in enumerate((bt, kt)):
                    b = 2 * (n % 2) + w
                    take(b)
                    for c in range(CT):
                        for o in H:
                            last = mm(ps[o, b, c * P:(c + 1) * P], src[o, c, n * CH:(n + 1) * CH], QR[o, c, n, 0:P])
                    last.then_inc(S["cm_ps"], 1)
                    readers[b] = [("cm_out", 2 * n + w + 1)]
                b = 4 + n % 2
                take(b)
                for w, src in enumerate((bt, kt)):
                    for c in range(CT):
                        for o in H:
                            last = mm(ps[o, b, w * 256 + c * CH:w * 256 + (c + 1) * CH], src[o, c, n * CH:(n + 1) * CH], ident[o, o])
                last.then_inc(S["tok_ps"], 1)
                readers[b] = [("tok_out", n + 1)]
            for n in range(NC):
                b = 6 + n % 2
                pe.wait_ge(S["x0t"], n + 1)
                take(b)
                for c in range(CT):
                    last = nc.tensor.transpose(ps[:, b, c * P:(c + 1) * P], XT[:, n, c, :], ident)
                last.then_inc(S["x0_ps"], 1)
                readers[b] = [("x0_out", n + 1)]
            nb = 0
            for l, _ in enumerate(LEVELS):
                ns = NC if l == 0 else NC - 1
                g0 = 0 if l == 0 else NC + (l - 1) * (NC - 1)
                if l == 0:
                    pe.wait_ge(S["x0_out"], NC)
                for n in range(ns):
                    b = nb % 8
                    nb += 1
                    take(b)
                    pe.wait_ge(S["m_ready"], g0 + n + 1)
                    for c in range(CT):
                        last = mm(ps[:, b, c * P:(c + 1) * P], Mk[:, (g0 + n) % 2, c, :], X[:, n, c, :])
                    last.then_inc(S["z_ps"], 1)
                    readers[b] = [("z_out", g0 + n + 1)]
                for n in range(ns):
                    b = nb % 8
                    nb += 1
                    take(b)
                    pe.wait_ge(S["z_out"], g0 + n + 1)
                    if l > 0:
                        pe.wait_ge(S["xt_out"], (0 if l == 1 else NC + (l - 2) * (NC - 1)) + n + 1)
                    for c in range(CT):
                        if l < len(LEVELS) - 1:
                            last = mm(ps[:, b, c * P:(c + 1) * P], XT[:, n, c, :], Zs[:, n, c, :])
                        else:
                            last = mm(ps[:, b, c * P:(c + 1) * P], Zs[:, n, c, :], XT[:, n, c, :])
                    last.then_inc(S["xz_ps"], 1)
                    readers[b] = [("x_add", g0 + n + 1)]
                if l < len(LEVELS) - 1:
                    for n in range(ns):
                        b = nb % 8
                        nb += 1
                        take(b)
                        pe.wait_ge(S["x_add"], g0 + n + 1)
                        for c in range(CT):
                            last = nc.tensor.transpose(ps[:, b, c * P:(c + 1) * P], X[:, n, c, :], ident)
                        last.then_inc(S["xt_ps"], 1)
                        readers[b] = [("xt_out", g0 + n + 1)]
            INV = NC + (len(LEVELS) - 1) * (NC - 1)
            pe.wait_ge(S["x_add"], INV)
            pe.wait_ge(S["tok_out"], NC)
            pe.wait_ge(S["cm_out"], 2 * NC)
            take(*range(8))

            def heads(f):
                for c in range(CT):
                    for h, o in enumerate(H):
                        last = f(c, h, o)
                return last

            for n in range(NC - 1):
                pe.wait_ge(S["s0_out"], n) if n else pe.wait_ge(S["lt_copied"], 3)

                def w_part(c, h, o):
                    mm(ps[o, 0, c * CH:(c + 1) * CH], QR[o, c, n, 0:CH], S0T[o, c, :], True, False)
                    return mm(ps[o, 0, c * CH:(c + 1) * CH], QK[o, n, c, 0:CH], Vtok[o, n, c, :], False, True)
                heads(w_part).then_inc(S["ws_ps"], 1)
                pe.wait_ge(S["ws_out"], n + 1)
                heads(lambda c, h, o: mm(ps[o, 1, c * CH:(c + 1) * CH], XT[o, n, c, o], Wsb[o, c, :])).then_inc(S["u_ps"], 1)
                pe.wait_ge(S["u_out"], n + 1)
                if n:
                    pe.wait_ge(S["y_out"], n)

                def y_part(c, h, o):
                    out = ps[o, 2, c * P:(c + 1) * P]
                    mm(out, S0T[o, c, :], QR[o, c, n, CH:3 * CH], True, False)
                    mm(out, Vtok[o, n, c, :], QK[o, n, c, CH:3 * CH], False, False)
                    return mm(out, Usb[o, c, :], QB[o, n, c, CH:3 * CH], False, True)
                heads(y_part).then_inc(S["ys_ps"], 1)
                pe.wait_ge(S["s_out"], n + 1)
                heads(lambda c, h, o: mm(ps[o, 3, c * CH:(c + 1) * CH], Ssb[o, c, :], ident[o, o])).then_inc(S["st_ps"], 1)
            pe.wait_ge(S["state_ld"], 16)
            pe.wait_ge(S["lt_copied"], 3 + 2 * NC + 1)
            R = [slice(0, NB * NT), slice(CH, CH + NB * NT)]
            for c in range(CT):
                for o in H:
                    last = mm(ps[o, 4 + c, :], QS[o, c, :],
                              S0s[o, c, :, :].rearrange("p b i -> p (b i)"))
                last.then_inc(S["sf_ps"], 1)
            n = NC - 1
            pe.wait_ge(S["s0_out"], NC - 1)
            heads(lambda c, h, o: mm(ps[o, 0, c * CH:(c + 1) * CH], QK[o, n, c, 0:CH], Vtok[o, n, c, :])).then_inc(S["ws_ps"], 1)
            pe.wait_ge(S["ws_out"], NC)
            heads(lambda c, h, o: mm(ps[o, 1, c * CH:(c + 1) * CH], XT[o, n, c, o], Wsb[o, c, :])).then_inc(S["u_ps"], 1)
            pe.wait_ge(S["u_out"], NC)
            pe.wait_ge(S["y_out"], NC - 1)

            def ys_part(c, h, o):
                out = ps[o, 2, c * 32:(c + 1) * 32]
                r = R[h]
                mm(out, Vtok[r, n, c, :], QK[r, n, c, CH:CH + 32], True, False)
                return mm(out, Usb[r, c, :], QB[r, n, c, CH:CH + 32], False, True)
            heads(ys_part)
            for c in range(CT):
                for h, o in enumerate(H):
                    r = slice(CH * h + 32, CH * h + 64)
                    last = mm(ps[o, 3, c * 32:(c + 1) * 32], WY[r, c, :], ident[r, r])
            last.then_inc(S["ys_ps"], 1)
            pe.wait_ge(S["um_ready"], 2)
            pe.wait_ge(S["wf"], CT)
            for c in range(CT):
                for h, o in enumerate(H):
                    r = R[h]
                    mm(ps[o, 4 + c, :], QB[r, n, c, 2 * CH:], Um[r, c, :, :].rearrange("p b i -> p (b i)"), True, False)
                    last = mm(ps[o, 4 + c, :], QK[r, n, c, 2 * CH:], Vm[r, c, :, :].rearrange("p b i -> p (b i)"), False, True)
            last.then_inc(S["sd_ps"], 1)
            pe.wait_ge(S["y_out"], NC)
            for c in range(CT):
                last = mm(ps[:, c, 0:TOK], mean64, yT[:, c, 0:TOK])
            last.then_inc(S["sum_ps"], 1)
            pe.wait_ge(S["snew"], 2)
            pe.wait_ge(S["sq_done"], 4)
            for c in range(CT):
                last = mm(ps[:, 4 + c, 0:TOK], mean64, t1[:, c, 0:TOK])
            last.then_inc(S["sum_ps"], 1)
            pe.wait_ge(S["cm1"], 1)
            pe.wait_ge(S["yc"], 1)
            for c in range(CT):
                last = mm(ps[:, 0, 0:TOK], ones, mix[:, CT + c, :], c == 0, c == CT - 1)
            last.then_inc(S["sum_ps"], 1)
            pe.wait_ge(S["sq_done"], 5)
            for c in range(CT):
                last = mm(ps[:, 1, 0:TOK], ones, t1[:, c, 0:TOK], c == 0, c == CT - 1)
            last.then_inc(S["sum_ps"], 1)
            pe.wait_ge(S["mix_done"], 1)
            for n in range(2):
                linear("w_out", n, mix, TOK, range(8), "wout_ps", 4 * n, lambda m: ("xres", m + 1))
            pe.wait_ge(S["sq_done"], 6)
            take(0)
            for k in range(KT):
                last = mm(ps[:, 0, 0:TOK], ones, mix[:, k, :], k == 0, k == KT - 1)
            last.then_inc(S["sum_ps"], 1)
            readers[0] = [("root", 6)]
            pe.wait_ge(S["h_done"], 2 * KT)
            for n in range(2):
                linear("w_q", n, hT, TOK, range(8), "q_ps", 4 * n, lambda m: ("q_out", m + 1))
            pe.wait_ge(S["q_out"], 8)
            take(*range(8))
            for u in range(8):
                h, t = u // 2, u % 2
                for k in range(2):
                    last = mm(ps[:, h, t * MEM:(t + 1) * MEM], q[:, 2 * h + k, t * P:(t + 1) * P], memK[:, 2 * h + k, :], k == 0, k == 1)
            last.then_inc(S["s_ps"], 1)
            for n in range(4):
                i, f = front_fill("cache_k", n)
                keys = part(ring, i * SLOT, 2, KT, MEM)
                pe.wait_ge(slot_in[i], 16 * (f + 1))
                for b in range(2):
                    for k in range(2):
                        for h in range(XH):
                            last = mm(ps[32 * h:32 * h + 32, 4 + n, b * MEM:(b + 1) * MEM], q[:, 2 * h + k, SEQ:TOK],
                                      keys[:, b, 2 * h + k, :], k == 0, k == 1)
                last.then_inc(S["sk_ps"], 1)
            pe.wait_ge(S["s_norm"], 1)
            for t in range(2):
                for m in range(2):
                    for h in range(XH):
                        last = nc.tensor.transpose(ps[:, 2 * m + t, h * P:(h + 1) * P], probs[:, 2 * h + t, m * P:(m + 1) * P], ident)
            last.then_inc(S["pt_ps"], 1)
            pe.wait_ge(S["ss_norm"], 1)
            for j in range(2 * NB):
                last = nc.tensor.transpose(ps[:, 4 + j // 4, (j % 4) * P:(j % 4 + 1) * P],
                                           ssam.rearrange("p b m -> p (b m)")[:, j * P:(j + 1) * P], ident)
            last.then_inc(S["st2_ps"], 1)
            pe.wait_ge(S["pt_out"], 1)
            for h in range(XH):
                for d in range(2):
                    for m in range(2):
                        last = mm(ps[:, h, d * SEQ:(d + 1) * SEQ].rearrange("p (t a) -> p t a", t=2), memV[:, m, (2 * h + d) * P:(2 * h + d + 1) * P],
                                  probsT.rearrange("p m (t h) a -> p m h t a", t=2)[:, m, h, :, :], m == 0, m == 1)
            last.then_inc(S["o_ps"], 1)
            pe.wait_ge(S["st2_out"], 1)
            for n in range(4):
                i, f = front_fill("cache_v", n)
                vals = part(ring, i * SLOT, 2, 2, D)
                pe.wait_ge(slot_in[i], 16 * (f + 1))
                for j in range(4):
                    for h in range(XH):
                        last = mm(ps[32 * h:32 * h + 32, 4, 0:MEM], ssamT[:, 4 * n + j, 32 * h:32 * h + 32],
                                  vals[:, j // 2, j % 2, h * MEM:(h + 1) * MEM], n == 0 and j == 0, n == 3 and j == 3)
                last.then_inc(S["sv_ps"], 1)
            pe.wait_ge(S["so_out"], 1)
            for d in range(2):
                last = nc.tensor.transpose(ps[:, 5, d * P:(d + 1) * P], osam[:, d * P:(d + 1) * P], ident)
            last.then_inc(S["so_ps"], 1)
            pe.wait_ge(S["o_out"], 1)
            pe.wait_ge(S["oT_out"], 1)
            for n in range(2):
                linear("w_o", n, mix, TOK, range(8), "wo_ps", 4 * n, lambda m: ("xres2", m + 1))
            pe.wait_ge(S["xres2"], KT)
            for j in range(TT):
                if j == 2:
                    pe.wait_ge(S["xt_out2"], 1)
                for k in range(KT):
                    last = nc.tensor.transpose(psP[j % 2][:, k * P:(k + 1) * P], xT[:, k, j * P:(j + 1) * P], ident)
                last.then_inc(S["xt_done"], 1)
            pe.wait_ge(S["xg_done"], 1)
            pe.wait_ge(S["small_in"], 16 * 7)
            for j in range(TT):
                for k in range(KT):
                    last = nc.tensor.matmul(psT[:, j * NE:(j + 1) * NE], xT[:, k, j * P:(j + 1) * P], w_r[:, k, :],
                                            start=(k == 0), stop=(k == KT - 1))
            last.then_inc(S["logit_ps"], 1)
            pe.wait_ge(S["mask_done"], 1)
            for j in range(TT):
                for i in range(j + 1):
                    nc.tensor.matmul(psG[:, j * NE:(j + 1) * NE], ones if i < j else before, mask[:, i, :],
                                     start=(i == 0), stop=(i == j))
            for i in range(TT):
                last = nc.tensor.matmul(psG[:, TT * NE:(TT + 1) * NE], ones, mask[:, i, :],
                                        start=(i == 0), stop=(i == TT - 1))
            last.then_inc(S["pos_ps"], 1)
            pe.wait_ge(S["comb_done"], 1)
            for j in range(TT):
                last = nc.tensor.transpose(psU[0:NE, j * P:(j + 1) * P], comb[:, j, 0:NE], ident)
            last.then_inc(S["combT_ps"], 1)
            pe.wait_ge(S["combT_out"], 1)
            pe.wait_ge(S["xt_out2"], 3)
            for j in range(TT):
                if j == 2:
                    pe.wait_ge(S["y_added"], 1)
                for n in range(2):
                    last = nc.tensor.matmul(psP[j % 2][:, n * 512:(n + 1) * 512], combT[:, j * P:(j + 1) * P],
                                            b_down[:, n * 512:(n + 1) * 512], start=True, stop=True)
                last.then_inc(S["ydown_ps"], 1)
            pe.wait_ge(S["route_ready"], 1)
            pe.wait_ge(S["h_ready"], 3)
            n = pe.value_load(load_i[0:1, 0:1], min_val=0, max_val=TOK)

            def product(ps, lhs, slots, fill, bias=None, done=None):
                for k in range(KT):
                    i = (FIRST_SLOT + slots + k // 4) % SLOTS
                    if k % 4 == 0:
                        pe.wait_ge(slot_in[i], 16 * (fill + 1 + FRONT_FILLS[i]))
                    for h in range(2):
                        last = nc.tensor.matmul(ps[CAP * h:CAP * h + CAP, :], lhs(k), part(ring, i * SLOT, 4, D)[:, k % 4, h * 512:(h + 1) * 512],
                                                start=(k == 0), stop=(k == KT - 1 and bias is None), skip_group_check=True)
                    if k % 4 == 3:
                        last.then_inc(slot_free[i], 1)
                if bias is not None:
                    for h in range(2):
                        last = nc.tensor.matmul(ps[CAP * h:CAP * h + CAP, :], bias[0], bias[1][:, h * 512:(h + 1) * 512],
                                                start=False, stop=True, skip_group_check=True)
                    last.then_inc(S[done], 1)

            def step(r, q, s):
                def in_xe(p):
                    return lambda k: xe[:, k, p, :]

                def in_hT(k):
                    return hexT[:, k % 4, k // 4, :]

                def turn_hid(st):
                    pe.wait_ge(S["hid_ready"], st + 1)
                    for j in range(4):
                        last = nc.tensor.transpose(psT[:, j * P:(j + 1) * P], hid[:, j * P:(j + 1) * P], ident)
                    last.then_inc(S["hT_done"], 1)
                    pe.wait_ge(S["hT_ready"], st + 1)

                def scatter(p):
                    pe.wait_ge(S["ye_ready"], 2 * s + p + 1)
                    for j in range(TT):
                        t = 3 * p + j
                        if t >= 2:
                            pe.wait_ge(S["y_added"], 6 * s + 3 + t - 1)
                        for h in range(2):
                            last = nc.tensor.matmul(psP[t % 2][:, h * 512:(h + 1) * 512],
                                                    gT[CAP * h:CAP * h + CAP, p, j * P:(j + 1) * P],
                                                    ye[CAP * h:CAP * h + CAP, :], start=True, stop=True)
                        last.then_inc(S["scat_done"], 1)

                pe.wait_ge(S["pick_ready"], r * (PAIRS + 1) + q + 1)
                pe.wait_ge(S["y_added"], 6 * s + 2)
                for k in range(KT):
                    for j in range(TT):
                        last = nc.tensor.matmul(psX[:, k * P:(k + 1) * P], h_tok[:, j, k * P:(k + 1) * P],
                                                pick[:, j, :, :], start=(j == 0), stop=(j == TT - 1))
                last.then_inc(S["disp_done"], 1)
                pe.wait_ge(S["y_added"], 6 * s + 3)
                for p in range(2):
                    for j in range(TT):
                        last = nc.tensor.transpose(psY[:, p * 512 + j * P:p * 512 + (j + 1) * P],
                                                   wpick[:, j, p, :, :].rearrange("t a c -> t (a c)"), ident)
                last.then_inc(S["wpickT_done"], 1)
                pe.wait_ge(S["one_ready"], s + 1)
                pe.wait_ge(S["xe_ready"], s + 1)
                product(psG, in_xe(0), 0, 2 * s, (one_e[:, 0, :], b_gate), "gate_done")
                product(psU, in_xe(0), 2, 2 * s, (one_e[:, 0, :], b_up), "up_done")
                pe.wait_ge(S["g_ready"], 2 * s + 1)
                product(psG, in_xe(1), 4, 2 * s, (one_e[:, 1, :], b_gate), "gate_done")
                turn_hid(2 * s)
                product(psD, in_hT, 0, 2 * s + 1)
                product(psU, in_xe(1), 2, 2 * s + 1, (one_e[:, 1, :], b_up), "up_done")
                pe.wait_ge(S["gT_ready"], s + 1)
                scatter(0)
                turn_hid(2 * s + 1)
                product(psD, in_hT, 4, 2 * s + 1)
                scatter(1)

            rounds(pe, n, step)

        @block.scalar
        def _(act):
            a = nc.scalar
            tell = counted(act)

            def copy(out, in_, scale=1.0):
                return a.activation(out, in_, ACT.Copy, scale=scale)

            act.wait_ge(S["x_in"], 16)
            tell("sq_done", a.activation(mix, xT[:, :, 0:TOK], ACT.Square), False)
            act.wait_ge(S["mem_in"], 16)
            tell("sq_done", a.activation(part(arena, 4352, KT, MEM), memT, ACT.Square), False)

            def root(sums, out, in_, scale, eps_at=None):
                act.wait_ge(S["sum_ps"], sums)
                bias = 0.0 if eps_at is None else eps[:, eps_at:eps_at + 1]
                tell("root", a.activation(out, in_, ACT.Sqrt, scale=scale, bias=bias), False)

            act.wait_ge(S["pool_i"], 9)
            root(1, rs[:, :], ps[:, 0, 0:TOK], 1.0 / D, 0)
            root(2, rs_mem, ps[:, 1, 0:MEM], 1.0 / D, 0)
            for i, c in enumerate(W_IN_ORDER[:RW]):
                act.wait_ge(S["p_ps"], i + 1)
                tell("p_out", copy(pext[:, c, 1:1 + SEQ], ps[:, i % 8, 0:SEQ]), False)
                tell("p_out", copy(pext[:, c, 1 + SEQ:].rearrange("p (b t) -> p b t", b=NB)[:, :, 1:],
                                   ps[:, i % 8, SEQ:TOK].rearrange("p (b t) -> p b t", b=NB)), False)
                if i == 5:
                    act.wait_ge(S["z_done"], 1)
                    tell("tl", a.activation(tlora[0:64, 0, :], z[0:64, 12, :], ACT.Tanh), False)
                    tell("tl", a.activation(tlora[:, 1, :], z[:, 13, :], ACT.Sigmoid), False)
            for j in range(CT):
                act.wait_ge(S["p_ps"], RW + 2 * j + 2)
                if j >= 2:
                    act.wait_ge(S["u_done"], 2 * (j - 1))
                else:
                    act.wait_ge(S["mem_h"], KT)
                tell("convgate", a.activation(tmp2[:, j % 2, 0:TOK], ps[:, (RW + 2 * j + 1) % 8, 0:TOK], ACT.Sigmoid), False)
            for c in range(CT):
                act.wait_ge(S["lora_ps"], c + 1)
                if c == 0:
                    act.wait_ge(S["const_in"], 32)
                tell("sw_done", a.activation(sw[:, c, :], ps[:, c, 0:TW], ACT.Sigmoid, bias=V("w0", c)), False)
            for c in range(CT):
                act.wait_ge(S["lora_ps"], CT + c + 1)
                tell("a_done", a.activation(iclr[:, c, :], ps[:, 4 + c, 0:TW], ACT.Sigmoid, bias=V("a0", c)), False)
            for c in range(CT):
                act.wait_ge(S["lora_ps"], 2 * CT + c + 1)
                tell("g_done", copy(gate[:, c, :], ps[:, c, 0:TW]), False)
            act.wait_ge(S["kk_done"], 1)
            tell("sq_done", a.activation(tmp, kk, ACT.Square), False)
            root(3, tmp, ps[:, 4:8, 0:TW], 64.0)
            act.wait_ge(S["scan"], 1)
            tell("exps", a.activation(Pm, cum, ACT.Exp, scale=-KAPPA), False)
            tell("exps", a.activation(Pinv, cum, ACT.Exp, scale=KAPPA), False)
            act.wait_ge(S["cumex"], 1)
            tell("exps", a.activation(Pex, sw, ACT.Exp, scale=-KAPPA), False)
            for m in range(KT):
                act.wait_ge(S["mk_ps"], m + 1)
                tell("mk_out", copy(memK[:, m, :], ps[:, m % 4, 0:MEM]), False)
            for b in range(4):
                act.wait_ge(S["mv_ps"], b + 1)
                tell("mv_out", copy(memV[:, b % 2, (b // 2) * 512:(b // 2 + 1) * 512], ps[:, b, :]), False)
            act.wait_ge(S["v_ps"], 1)
            act.wait_ge(S["mix_b"], 1)
            tell("v_out", copy(Vtok.rearrange("p n c i -> p (n c i)"), ps[:, 4:7, :].rearrange("p b f -> p (b f)")[:, 0:NC * 256]))
            for n in range(NC):
                act.wait_ge(S["tok_ps"], n + 1)
                src = ps[:, 4 + n % 2, :].rearrange("p (w c j) -> p w c j", w=2, c=CT)
                copy(QB[:, n, :, 2 * CH:], src[:, 0, :, :])
                tell("tok_out", copy(QK[:, n, :, 2 * CH:], src[:, 1, :, :]), False)
            for n in range(NC):
                act.wait_ge(S["x0_ps"], n + 1)
                tell("x0_out", copy(X[:, n, :, :].rearrange("p c t -> p (c t)"), ps[:, 6 + n % 2, :]), False)
            nb = 0
            for l, _ in enumerate(LEVELS):
                ns = NC if l == 0 else NC - 1
                g0 = 0 if l == 0 else NC + (l - 1) * (NC - 1)
                for n in range(ns):
                    act.wait_ge(S["z_ps"], g0 + n + 1)
                    if l:
                        act.wait_ge(S["xz_ps"], (0 if l == 1 else NC + (l - 2) * (NC - 1)) + n + 1)
                    tell("z_out", copy(Zs[:, n, :, :].rearrange("p c t -> p (c t)"), ps[:, nb % 8, :]), False)
                    nb += 1
                nb += ns
                if l < len(LEVELS) - 1:
                    for n in range(ns):
                        act.wait_ge(S["xt_ps"], g0 + n + 1)
                        tell("xt_out", copy(XT[:, n, :, :].rearrange("p c t -> p (c t)"), ps[:, nb % 8, :]), False)
                        nb += 1
            for n in range(NC - 1):
                act.wait_ge(S["ws_ps"], n + 1)
                tell("ws_out", copy(Wsb.rearrange("p c i -> p (c i)"), ps[:, 0, 0:256]), False)
            act.wait_ge(S["yc"], 1)
            tell("sq_done", a.activation(t1[:, :, 0:TOK], yT[:, :, 0:TOK], ACT.Square), False)
            root(6, t2[:, :, 0:TOK], ps[:, 4:8, 0:TOK], 1.0, 1)
            act.wait_ge(S["cc"], 1)
            tell("sq_done", a.activation(t1[:, :, 0:TOK], mix[:, CT:, :], ACT.Square), False)
            root(8, rs[:, :], ps[:, 1, 0:TOK], 1.0 / (CT * P), 0)
            act.wait_ge(S["cnorm"], CT)
            tell("csig", a.activation(t1[:, :, 0:TOK], mix[:, CT:, :], ACT.Sigmoid), False)
            act.wait_ge(S["xres"], KT)
            tell("sq_done", a.activation(mix, xT[:, :, 0:TOK], ACT.Square), False)
            root(9, rs[:, :], ps[:, 0, 0:TOK], 1.0 / D, 0)
            for m in range(KT):
                act.wait_ge(S["q_ps"], m + 1)
                tell("q_out", copy(q[:, m, :], ps[:, m, 0:TOK]), False)
            act.wait_ge(S["s_max"], 1)
            for u in range(8):
                tell("s_exp", a.activation(probs[:, u, :], ps[:, u // 2, (u % 2) * MEM:(u % 2 + 1) * MEM], ACT.Exp,
                                           scale=1.0 / 16, bias=amax[:, u:u + 1], accum_out=asum[:, u:u + 1]), False)
            act.wait_ge(S["ss_max"], 1)
            tell("ss_exp", a.activation(ssam, ssam, ACT.Exp, scale=1.0 / 16, bias=amax[:, 8:9], accum_out=asum[:, 8:9]), False)
            act.wait_ge(S["pt_ps"], 1)
            tell("pt_out", copy(probsT.rearrange("p m u a -> p (m u a)"), ps[:, 0:4, :].rearrange("p b f -> p (b f)")), False)
            act.wait_ge(S["st2_ps"], 1)
            tell("st2_out", copy(ssamT.rearrange("p j a -> p (j a)"), ps[:, 4:8, :].rearrange("p b f -> p (b f)")), False)
            act.wait_ge(S["o_ps"], 1)
            tell("o_out", copy(mix[:, :, 0:SEQ], ps[:, 0:4, :].rearrange("p h (d t) -> p (h d) t", d=2)), False)
            act.wait_ge(S["sv_ps"], 4)
            tell("so_out", copy(osam, ps[:, 4, 0:MEM]), False)
            act.wait_ge(S["so_ps"], 1)
            for d in range(2):
                last = copy(mix.rearrange("p (h d) t -> p h d t", d=2)[:, :, d, SEQ:TOK],
                            ps[:, 5, d * P:(d + 1) * P].rearrange("p (h t) -> p h t", h=XH))
            tell("oT_out", last, False)
            for j in range(TT):
                act.wait_ge(S["xt_done"], j + 1)
                nc.scalar.activation(x_tok[:, j, :], psP[j % 2][:, :], ACT.Copy).then_inc(S["xt_out2"], 1)
            act.wait_ge(S["xt_out2"], 3)
            for j in range(TT):
                nc.scalar.activation(h_tok[:, j, :], x_tok[:, j, :], ACT.Square,
                                     accum_out=ssq[:, j:j + 1]).then_inc(S["ssq_done"], 1)
            act.wait_ge(S["ssq_done"], 3)
            tell("root", a.activation(ssq, ssq, ACT.Sqrt, scale=1.0 / D, bias=eps[:, 0:1]), False)
            act.wait_ge(S["max_done"], 1)
            for j in range(TT):
                nc.scalar.activation(comb[:, j, 0:NE], logit[:, j, :], ACT.Exp, bias=ntop[:, j:j + 1]).then_inc(S["exp_done"], 1)
            act.wait_ge(S["combT_ps"], 1)
            nc.scalar.activation(combT[:, :], psU[0:NE, 0:TT * P], ACT.Copy).then_inc(S["combT_out"], 1)
            act.wait_ge(S["route_ready"], 1)
            n = act.value_load(load_i[0:1, 0:1], min_val=0, max_val=TOK)

            def step(r, q, s):
                act.wait_ge(S["disp_done"], s + 1)
                nc.scalar.activation(xe[:, :, :, :].rearrange("p k a c -> p (k a c)"), psX, ACT.Copy).then_inc(S["xe_ready"], 1)
                act.wait_ge(S["wpickT_done"], s + 1)
                nc.scalar.activation(gT[:, :, :], psY.rearrange("p (a t) -> p a t", a=2)[:, :, 0:TT * P], ACT.Copy).then_inc(S["gT_ready"], 1)
                for p in range(2):
                    st = 2 * s + p
                    act.wait_ge(S["g_ready"], st + 1)
                    nc.scalar.activation(sig, gmin, ACT.Sigmoid, scale=1.702).then_inc(S["sig_ready"], 1)
                    act.wait_ge(S["hT_done"], st + 1)
                    nc.scalar.activation(hexT.rearrange("p a b c -> p (a b c)"), psT, ACT.Copy).then_inc(S["hT_ready"], 1)
                    act.wait_ge(slot_free[(FIRST_SLOT + 1 + 4 * p) % SLOTS], 2 * s + 2)
                    nc.scalar.activation(ye, psD, ACT.Copy).then_inc(S["ye_ready"], 1)

            rounds(act, n, step)
            act.wait_ge(S["fin_ssq"], 1)
            for j in range(TT):
                nc.scalar.activation(h_tok[:, j, :], y[:, j, :], ACT.Square,
                                     accum_out=ssq[:, j:j + 1]).then_inc(S["ssq_done"], 1)
            act.wait_ge(S["ssq_done"], 6)
            tell("root", a.activation(ssq, ssq, ACT.Sqrt, scale=1.0 / D, bias=eps[:, 0:1]), False)

        @block.vector
        def _(dve):
            v = nc.vector
            tell = counted(dve)

            def tt(out, x, y, op):
                return v.tensor_tensor(out, x, y, op)

            def stt(out, x, s, y, o0, o1):
                return v.scalar_tensor_tensor(out, x, s, y, o0, o1)

            def link(ins):
                tell("dve_c", ins)

            MUL, ADD, SUB = ALU.mult, ALU.add, ALU.subtract
            dve.wait_ge(S["const_in"], 32)
            dve.wait_ge(S["x_in"], 16)

            def norm(n, src, out, rs, w, g, done):
                dve.wait_ge(S["root"], n)
                link(v.reciprocal(rs, rs))
                for k in range(KT):
                    tell(done, stt(out[:, k, 0:w], src[:, k, 0:w], V(g, k), rs, MUL, MUL), False)

            norm(1, xT, hT, rs[:, :], TOK, "g_mix", "h_done")
            dve.wait_ge(S["h_done"], KT)
            norm(2, memT, memT, rs_mem, MEM, "g_mem", "mem_h")

            def shift(lo, hi):
                pe3 = pext[:, lo:hi, 1 + SEQ:].rearrange("p c (b t) -> p c b t", b=NB)
                tell("dve_c", tt(z[:, lo:hi, 0:SEQ], pext[:, lo:hi, 0:SEQ], pext[:, lo:hi, 1:1 + SEQ], SUB), False)
                link(tt(z[:, lo:hi, SEQ:TOK].rearrange("p c (b t) -> p c b t", b=NB), pe3[:, :, :, 0:NT], pe3[:, :, :, 1:], SUB))
                for c in range(lo, hi):
                    stt(z[:, c, 0:SEQ], z[:, c, 0:SEQ], V("mu", c), pext[:, c, 1:1 + SEQ], MUL, ADD)
                    zs = z[:, c, SEQ:TOK].rearrange("p (b t) -> p b t", b=NB)
                    last = stt(zs, zs, V("mu", c), pe3[:, c - lo, :, 1:], MUL, ADD)
                tell("z_done", last)

            dve.wait_ge(S["p_out"], 4)
            shift(12, 14)
            dve.wait_ge(S["p_out"], 12)
            shift(4, 8)
            for c in range(CT):
                last = v.tensor_scalar(kk[:, c, :], z[:, 4 + c, :], V("k_k", c), None, MUL)
            tell("kk_done", last)
            dve.wait_ge(S["p_out"], 20)
            shift(0, 4)
            dve.wait_ge(S["p_out"], 28)
            shift(8, 12)
            dve.wait_ge(S["ext_ld"], 64)
            for j in range(CT):
                dve.wait_ge(S["convgate"], j + 1)
                b = (RW + 2 * j) % 8
                tell("u_done", tt(ext[:, j, TAPS - 1:TAPS - 1 + SEQ], ps[:, b, 0:SEQ], tmp2[:, j % 2, 0:SEQ], MUL), False)
                tell("u_done", tt(ext[:, j, TAPS - 1 + SEQ:].rearrange("p (b t) -> p b t", b=NB)[:, :, TAPS - 1:],
                                  ps[:, b, SEQ:TOK].rearrange("p (b t) -> p b t", b=NB),
                                  tmp2[:, j % 2, SEQ:TOK].rearrange("p (b t) -> p b t", b=NB), MUL), j == CT - 1)
            dve.wait_ge(S["sw_done"], CT)
            flat = "p c t -> p (c t)"
            tell("scan", v.tensor_tensor_scan(cum.rearrange(flat), rmask.rearrange(flat), sw.rearrange(flat), 0.0, MUL, ADD))
            tell("cumex", tt(sw, cum, sw, SUB))
            dve.wait_ge(S["a_done"], CT)
            for c in range(CT):
                last = v.tensor_scalar(kmod[:, c, :], iclr[:, c, :], 1.0, V("k_a", c), SUB, MUL)
            link(last)
            link(stt(kmod, kmod, 1.0, z[:, 4:8, :], ADD, MUL))
            dve.wait_ge(S["root"], 3)
            link(v.tensor_scalar(tmp, tmp, 1e-12, None, ALU.max))
            link(v.reciprocal(tmp, tmp))
            link(tt(kk, kk, tmp, MUL))
            dve.wait_ge(S["exps"], 3)
            QRv = QR.rearrange("p c n t -> p (c n) t")
            cn = "p c (n t) -> p (c n) t"
            dve.wait_ge(S["lora_ps"], 3 * CT)
            dve.wait_ge(S["pool_i"], 11)
            tt(iclr, kk, iclr, MUL)
            stt(QRv[:, :, 0:CH], kk.rearrange(cn, t=CH), -1.0, Pex.rearrange(cn, t=CH), MUL, MUL)
            tt(QRv[:, :, CH:P], z[:, 0:4, :].rearrange(cn, t=CH), Pm.rearrange(cn, t=CH), MUL)
            tt(kt, kmod, Pinv, MUL)
            for c in range(CT):
                last = stt(tmp[:, c, :], z[:, c, :], V("r_k", c), kmod[:, c, :], MUL, MUL)
            link(last)
            tell("prep", tt(bt, iclr, Pinv, MUL))
            dve.wait_ge(S["sum_ps"], 4)
            tell("mix_b", stt(mix[:, 0:CT, :], ps[:, 4:8, 0:TOK], 64.0, z[:, 8:12, 0:TOK], MUL, MUL))

            def conv(lo, hi):
                for k in range(lo, hi):
                    for c in range(CT):
                        w = V("dw_w", c * TAPS + k)
                        xp = ext[:, c, k:k + SEQ]
                        xs = ext[:, c, TAPS - 1 + SEQ:].rearrange("p (b t) -> p b t", b=NB)[:, :, k:k + NT]
                        yp = mix[:, CT + c, 0:SEQ]
                        ys = mix[:, CT + c, SEQ:TOK].rearrange("p (b t) -> p b t", b=NB)
                        if k == 0:
                            v.tensor_scalar(yp, xp, w, V("dw_b", c), MUL, ADD)
                            last = v.tensor_scalar(ys, xs, w, V("dw_b", c), MUL, ADD)
                        else:
                            dve.wait_ge(S["conv"], CT * (k - 1) + c + 1)
                            stt(yp, xp, w, yp, MUL, ADD)
                            last = stt(ys, xs, w, ys, MUL, ADD)
                        last.then_inc(S["conv"], 1)

            dve.wait_ge(S["pool_i"], 9)
            conv(0, 10)
            for n in range(NC):
                keep = C("causal" if n < NC - 1 else "causal_s").unsqueeze(1).broadcast_to([P, CT, P])
                for w, dst in enumerate((QB, QK)):
                    dve.wait_ge(S["cm_ps"], 2 * n + w + 1)
                    tell("cm_out", tt(dst[:, n, :, 0:P], ps[:, 2 * (n % 2) + w, :].rearrange("p (c t) -> p c t", c=CT), keep, MUL), False)

            def level(l):
                return C("levels")[:, l * 64:(l + 1) * 64].unsqueeze(1).broadcast_to([P, 2 * CT, 64])

            halves = "p c (h t) -> p (c h) t"
            for n in range(NC):
                dve.wait_ge(S["lt_copied"], 3 + 2 * (n + 1))
                link(tt(XT[:, n, :, :].rearrange(halves, h=2), LT[:, n, :, :].rearrange(halves, h=2), level(0), MUL))
                tell("x0t", tt(XT[:, n, :, :], XT[:, n, :, :], ident.unsqueeze(1).broadcast_to([P, CT, P]), ADD), False)
            nb = 0
            for l, _ in enumerate(LEVELS):
                ns = NC if l == 0 else NC - 1
                g0 = 0 if l == 0 else NC + (l - 1) * (NC - 1)
                for n in range(ns):
                    g = g0 + n
                    if g >= 2:
                        dve.wait_ge(S["z_ps"], g - 1)
                    tell("m_ready", tt(Mk[:, g % 2, :, :].rearrange(halves, h=2), LT[:, n, :, :].rearrange(halves, h=2), level(l + 1), MUL), False)
                conv(10 + 4 * l, 14 + 4 * l)
                nb += ns
                for n in range(ns):
                    dve.wait_ge(S["xz_ps"], g0 + n + 1)
                    at = (X if l < len(LEVELS) - 1 else XT)[:, n, :, :].rearrange("p c t -> p (c t)")
                    tell("x_add", tt(at, at, ps[:, nb % 8, :], ADD), False)
                    nb += 1
                nb += ns
            conv(30, TAPS)
            dve.wait_ge(S["conv"], CT * TAPS)
            tell("cm1", v.tensor_copy(amax[:, 0:1], V("mu")))
            dve.wait_ge(S["pc_done"], 2)
            half4 = ps[:, 2, :].rearrange("p (c t) -> p c t", c=CT)
            for n in range(NC - 1):
                dve.wait_ge(S["u_ps"], n + 1)
                tell("u_out", v.tensor_copy(Usb.rearrange("p c i -> p (c i)"), ps[:, 1, 0:256]), False)
                dve.wait_ge(S["ys_ps"], n + 1)
                tell("s_out", v.tensor_copy(Ssb, half4[:, :, CH:]), False)
                tell("y_out", v.tensor_copy(yT[:, :, n * CH:(n + 1) * CH], half4[:, :, 0:CH]), False)
                dve.wait_ge(S["st_ps"], n + 1)
                tell("s0_out", tt(S0T, ps[:, 3, 0:256].rearrange("p (c i) -> p c i", c=CT),
                                  PC[:, :, n:n + 1].broadcast_to([P, CT, CH]), MUL), False)
            own = C("of_sample").unsqueeze(2).broadcast_to([P, NB, CH])
            for c in range(CT):
                dve.wait_ge(S["sf_ps"], c + 1)
                tell("wf", tt(Wf[:, c, :, :], ps[:, 4 + c, :].rearrange("p (b i) -> p b i", b=NB), own, MUL))
            link(v.tensor_reduce(WY, Wf.rearrange("p c b i -> p c i b"), AX.X, ADD))
            dve.wait_ge(S["ws_ps"], NC)
            tt(Wsb.rearrange("p c i -> p (c i)"), ps[:, 0, 0:256], WY.rearrange("p c i -> p (c i)"), ADD).then_inc(S["ws_out"], 1)
            dve.wait_ge(S["u_ps"], NC)
            tell("u_out", v.tensor_copy(Usb.rearrange("p c i -> p (c i)"), ps[:, 1, 0:256]))
            for c in range(CT):
                last = tt(Um[:, c, :, :], Usb[:, c, :].unsqueeze(1).broadcast_to([P, NB, CH]), own, MUL)
            tell("um_ready", last, False)
            for c in range(CT):
                last = tt(Vm[:, c, :, :], Vtok[:, NC - 1, c, :].unsqueeze(1).broadcast_to([P, NB, CH]), own, MUL)
            tell("um_ready", last, False)
            dve.wait_ge(S["ys_ps"], NC)
            ysam = yT[:, :, SEQ:TOK]
            link(v.tensor_copy(ysam, ps[:, 2, 0:128].rearrange("p (c t) -> p c t", c=CT)))
            tell("y_out", tt(ysam, ysam, ps[:, 3, 0:128].rearrange("p (c t) -> p c t", c=CT), ADD))
            dve.wait_ge(S["sd_ps"], 1)
            S0f = S0s.rearrange("p c b i -> p c (b i)")
            tell("snew", tt(S0f, S0f, ps[:, 4:8, :], ADD))
            S0c = S0s.rearrange("p c b i -> p (c b) i")
            tell("snew", tt(S0c, S0c, PCs[:, :, :].rearrange("p c b -> p (c b)").unsqueeze(2).broadcast_to([P, CT * NB, CH]), MUL))
            y0 = yT[:, :, 0:TOK]
            dve.wait_ge(S["sum_ps"], 5)
            tell("yc", tt(y0, y0, ps[:, 0:4, 0:TOK], SUB))
            rsb = rs[:, :].unsqueeze(1).broadcast_to([P, CT, TOK])
            cv = mix[:, CT:, :]
            dve.wait_ge(S["sum_ps"], 7)
            link(v.tensor_scalar(rs[:, :], ps[:, 0, 0:TOK], 1.0 / (CT * P), None, MUL))
            tell("cc", tt(cv, cv, rsb, SUB))
            dve.wait_ge(S["root"], 4)
            link(v.reciprocal(t2[:, :, 0:TOK], t2[:, :, 0:TOK]))
            link(tt(y0, y0, t2[:, :, 0:TOK], MUL))
            for c in range(CT):
                last = v.tensor_scalar(y0[:, c, :], y0[:, c, :], V("gn_g", c), V("gn_b", c), MUL, ADD)
            link(last)
            link(tt(y0, y0, mix[:, 0:CT, :], ADD))
            link(tt(mix[:, 0:CT, :], y0, gate[:, :, 0:TOK], MUL))
            dve.wait_ge(S["root"], 5)
            link(v.reciprocal(rs[:, :], rs[:, :]))
            link(tt(cv, cv, rsb, MUL))
            for c in range(CT):
                tell("cnorm", v.tensor_scalar(cv[:, c, :], cv[:, c, :], V("cln_g", c), V("cln_b", c), MUL, ADD), c == CT - 1)
            dve.wait_ge(S["csig"], 1)
            tell("mix_done", tt(cv, cv, t1[:, :, 0:TOK], MUL))
            for m in range(KT):
                dve.wait_ge(S["wout_ps"], m + 1)
                tell("xres", tt(xT[:, m, 0:TOK], xT[:, m, 0:TOK], ps[:, m, 0:TOK], ADD))
            norm(6, xT, hT, rs[:, :], TOK, "g_x", "h_done")
            dve.wait_ge(S["s_ps"], 1)
            link(v.tensor_reduce(amax[:, 0:8], ps[:, 0:4, :].rearrange("p h (t m) -> p (h t) m", t=2), AX.X, ALU.max))
            tell("s_max", v.tensor_scalar(amax[:, 0:8], amax[:, 0:8], -1.0 / 16, None, MUL))
            dve.wait_ge(S["s_exp"], 8)
            link(v.reciprocal(asum[:, 0:8], asum[:, 0:8]))
            tell("s_norm", tt(probs, probs, asum[:, 0:8].unsqueeze(2).broadcast_to([P, 8, MEM]), MUL))
            dve.wait_ge(S["sk_ps"], 4)
            dve.wait_ge(S["osent"], 16 * 3)
            link(tt(ssam, ps[:, 4:8, :].rearrange("p n (b m) -> p (n b) m", b=2),
                              C("not_sample").unsqueeze(2).broadcast_to([P, NB, MEM]), ADD))
            flat_s = ssam.rearrange("p b m -> p (b m)")
            link(v.tensor_reduce(amax[:, 8:9], flat_s, AX.X, ALU.max))
            tell("ss_max", v.tensor_scalar(amax[:, 8:9], amax[:, 8:9], -1.0 / 16, None, MUL))
            dve.wait_ge(S["ss_exp"], 1)
            link(v.reciprocal(asum[:, 8:9], asum[:, 8:9]))
            tell("ss_norm", v.tensor_scalar(flat_s, flat_s, asum[:, 8:9], None, MUL))
            for m in range(KT):
                dve.wait_ge(S["wo_ps"], m + 1)
                tell("xres2", tt(xT[:, m, 0:TOK], xT[:, m, 0:TOK], ps[:, m, 0:TOK], ADD), False)
            link = Chain(dve, S["dve_m"])
            dve.wait_ge(S["xres2"], KT)
            dve.wait_ge(S["xt_done"], 3)
            for k in range(KT):
                last = nc.vector.tensor_scalar(xT[:, k, :], xT[:, k, :], V("g_moe", k), None, ALU.mult)
            last.then_inc(S["xg_done"], 1)
            dve.wait_ge(S["root"], 7)
            link(nc.vector.reciprocal(rstd, ssq))
            dve.wait_ge(S["logit_ps"], 1)
            for j in range(TT):
                nc.vector.scalar_tensor_tensor(logit[:, j, :], psT[:, j * NE:(j + 1) * NE], rstd[:, j:j + 1], b_r,
                                               ALU.mult, ALU.add).then_inc(S["dve_m"], 1)
            link.n += 3
            dve.wait_ge(S["dve_m"], link.n)
            for j in range(TT):
                nc.vector.max(top8[:, j, :], logit[:, j, :]).then_inc(S["dve_m"], 1)
            link.n += 3
            dve.wait_ge(S["dve_m"], link.n)
            nc.vector.tensor_scalar(ntop, top8[:, :, 0], -1.0, None, ALU.mult).then_inc(S["max_done"], 1)
            v4 = top8[:, :, 3].unsqueeze(2).broadcast_to([P, TT, NE])
            nc.vector.tensor_tensor(over[:, :, :], logit[:, :, :], v4, ALU.is_gt).then_inc(S["dve_m"], 1)
            nc.vector.tensor_tensor(tie[:, :, :], logit[:, :, :], v4, ALU.is_equal).then_inc(S["dve_m"], 1)
            link.n += 2
            dve.wait_ge(S["dve_m"], link.n)
            nc.vector.tensor_reduce(need, over[:, :, :], AX.X, ALU.add).then_inc(S["dve_m"], 1)
            dve.wait_ge(S["pool_c"], 1)
            for j in range(TT):
                nc.vector.tensor_tensor_scan(tiecum[:, j, :], zero, tie[:, j, :], 0.0, ALU.mult, ALU.add).then_inc(S["dve_m"], 1)
            link.n += 4
            dve.wait_ge(S["dve_m"], link.n)
            link(nc.vector.tensor_scalar(need, need, -1.0, 4.0, ALU.mult, ALU.add))
            for j in range(TT):
                link(nc.vector.scalar_tensor_tensor(tie[:, j, :], tiecum[:, j, :], need[:, j:j + 1], tie[:, j, :], ALU.is_le, ALU.mult))
            link(nc.vector.tensor_tensor(mask[:, :, :], over[:, :, :], tie[:, :, :], ALU.add))
            nc.vector.tensor_tensor(mask[:, :, :], mask[:, :, :], valid.unsqueeze(2).broadcast_to([P, TT, NE]), ALU.mult).then_inc(S["mask_done"], 1)
            dve.wait_ge(S["mask_done"], 1)
            dve.wait_ge(S["exp_done"], 3)
            link(nc.vector.tensor_tensor(comb[:, :, 0:NE], comb[:, :, 0:NE], mask[:, :, :], ALU.mult))
            link(nc.vector.tensor_reduce(esum, comb[:, :, 0:NE], AX.X, ALU.add))
            link(nc.vector.tensor_scalar(esum, esum, 1e-30, None, ALU.max))
            link(nc.vector.reciprocal(esum, esum))
            nc.vector.tensor_tensor(comb[:, :, 0:NE], comb[:, :, 0:NE], esum.unsqueeze(2).broadcast_to([P, TT, NE]), ALU.mult).then_inc(S["comb_done"], 1)
            dve.wait_ge(S["comb_done"], 1)
            dve.wait_ge(S["pos_ps"], 1)
            link(nc.vector.scalar_tensor_tensor(pos[:, :, 0:NE], psG[:, 0:TT * NE].rearrange("p (j e) -> p j e", e=NE), 1.0,
                                           mask[:, :, :], ALU.add, ALU.mult))
            nc.vector.tensor_scalar(pos[:, :, 0:NE], pos[:, :, 0:NE], CAP - 1.0, None, ALU.add).then_inc(S["dve_m"], 1)
            nc.vector.tensor_reduce(load, psG[:, TT * NE:(TT + 1) * NE], AX.X, ALU.max).then_inc(S["dve_m"], 1)
            link.n += 2
            dve.wait_ge(S["dve_m"], link.n)
            nc.vector.tensor_copy(load_i[:, :], load).then_inc(S["route_ready"], 1)
            for j in range(TT):
                nc.vector.scalar_tensor_tensor(h_tok[:, j, :], x_tok[:, j, :], rstd[:, j:j + 1], g_row,
                                               ALU.mult, ALU.mult).then_inc(S["h_ready"], 1)
            dve.wait_ge(S["h_ready"], 3)
            for j in range(TT):
                dve.wait_ge(S["ydown_ps"], j + 1)
                nc.vector.tensor_tensor(y[:, j, :], x_tok[:, j, :], psP[j % 2][:, :], ALU.add).then_inc(S["y_added"], 1)
            dve.wait_ge(S["route_ready"], 1)
            n = dve.value_load(load_i[0:1, 0:1], min_val=0, max_val=TOK)
            base = link.n

            PICKS, LINKS = 2, 4
            per_round = (PAIRS + 1) * PICKS + PAIRS * LINKS

            def make_pick(q, link):
                for p in range(2):
                    nc.vector.tensor_tensor(pick[:, :, p, :], iota[:, 0:CAP].unsqueeze(1).broadcast_to([P, TT, CAP]),
                                            pos[:, :, bass.ds(2 * q + p, 1)].broadcast_to([P, TT, CAP]), ALU.is_equal).then_inc(S["dve_m"], 1)
                link.n += 2
                dve.wait_ge(S["dve_m"], link.base + link.n)
                for p in range(2):
                    for h in range(2):
                        last = nc.vector.tensor_tensor(wpick[:, :, p, h, :], pick[:, :, p, :],
                                                       comb[:, :, bass.ds(2 * q + p, 1)].broadcast_to([P, TT, CAP]), ALU.mult)
                last.then_inc(S["pick_ready"], 1)

            def next_round(r):
                nc.vector.tensor_scalar(pos[:, :, 0:NE], pos[:, :, 0:NE], -float(CAP), None, ALU.add).then_inc(S["round_pos"], 1)
                dve.wait_ge(S["round_pos"], r + 1)
                make_pick(0, Chain(dve, S["dve_m"], base + r * per_round))

            def step(r, q, s):
                link = Chain(dve, S["dve_m"], base + r * per_round + PICKS + q * (PICKS + LINKS))
                for p in range(2):
                    last = nc.vector.tensor_copy(one_e[:, p, :], ident[0:NE, bass.ds(2 * q + p, 1)].broadcast_to([NE, CAP]))
                last.then_inc(S["one_ready"], 1)

                def gate(p):
                    dve.wait_ge(S["gate_done"], 2 * s + p + 1)
                    nc.vector.tensor_scalar(gmin, psG, 7.0, None, ALU.min).then_inc(S["g_ready"], 1)

                def swiglu(p):
                    dve.wait_ge(S["g_ready"], 2 * s + p + 1)
                    dve.wait_ge(S["up_done"], 2 * s + p + 1)
                    link(nc.vector.tensor_scalar(ug, psU, 7.0, -7.0, ALU.min, ALU.max))
                    link(nc.vector.scalar_tensor_tensor(ug, ug, 1.0, gmin, ALU.add, ALU.mult))
                    dve.wait_ge(S["sig_ready"], 2 * s + p + 1)
                    nc.vector.tensor_tensor(hid, ug, sig, ALU.mult).then_inc(S["hid_ready"], 1)

                gate(0)
                swiglu(0)
                gate(1)
                dve.wait_ge(S["wpickT_done"], s + 1)
                make_pick(q + 1, link)
                swiglu(1)
                for t in range(2 * TT):
                    dve.wait_ge(S["scat_done"], 6 * s + t + 1)
                    nc.vector.tensor_tensor(y[:, t % TT, :], y[:, t % TT, :], psP[t % 2][:, :], ALU.add).then_inc(S["y_added"], 1)

            rounds(dve, n, step, next_round)
            nc.vector.tensor_copy(load, load_i[:, :]).then_inc(S["fin_ssq"], 1)
            dve.wait_ge(S["root"], 8)
            nc.vector.reciprocal(rstd, ssq).then_inc(S["fin_recip"], 1)
            dve.wait_ge(S["fin_recip"], 1)
            for j in range(TT):
                nc.vector.scalar_tensor_tensor(h_tok[:, j, :], y[:, j, :], rstd[:, j:j + 1], gf_row, ALU.mult, ALU.mult).then_inc(S["out_ready"], 1)


def constants():
    import numpy as np
    c = np.zeros((P, CONSTW), np.float32)

    def put(name, a):
        at, n = CONST[name]
        c[:, at:at + n] = a

    p = np.arange(P)[:, None]
    t = np.arange(P)[None, :]
    put("ident", p == t)
    put("ones", 1)
    put("before", p < t)
    put("mean64", (p // CH == t // CH) / CH)
    put("iota", np.arange(CAP)[None, :])
    put("istack", p % CH == np.arange(CH)[None, :])
    s = p % CH
    u = t % CH
    causal = np.where(t < CH, s < u, s <= u)
    put("causal", causal)
    put("causal_s", causal & (s // NT == u // NT) & (s < NB * NT) & (u < NB * NT))
    u = np.arange(CH)[None, :]
    put("levels", np.concatenate([(s // (2 * b) == u // (2 * b)) & (s // b < u // b) for b in (1,) + LEVELS], axis=1))
    put("of_sample", p % (NB * NT) // NT == np.arange(NB)[None, :])
    put("not_sample", np.where(p % (NB * NT) // NT == np.arange(NB)[None, :], 0, -1e30))
    put("valid", np.arange(TT)[None, :] * P + p < TOK)
    return c


def kernel(**inputs):
    import numpy as np
    import concourse.bacc as bacc
    from concourse.bass_utils import run_bass_kernel_spmd as run
    a = {k: np.asarray(v) for k, v in inputs.items()}
    f = np.float32

    def cols(v):
        return v.reshape(-1, P).T

    def halves(w):
        return np.stack([w[:, n * 512:(n + 1) * 512].reshape(KT, P, 512).transpose(1, 0, 2).reshape(P, -1) for n in range(2)])

    xT = np.zeros((P, KT, TT * P), f)
    xT[:, :, 0:TOK] = np.concatenate([a["x_prompt"][0], a["x_sample"].reshape(-1, D)]).T.reshape(KT, P, TOK).transpose(1, 0, 2)
    w_in = a["w_in"][0].reshape(KT, P, -1, P)
    w_in = w_in[:, :, list(W_IN_ORDER), :]
    fills = [w_in[:, :, 4 * n:4 * n + 4, :].transpose(1, 0, 2, 3).reshape(P, -1) for n in range(6)]
    vec = np.concatenate([cols(a[n][0]) for n in ("g_mix", "g_mem", "g_xattn", "g_moe", "mu_shift", "w0", "a0", "k_k", "k_a")]
                         + [cols(a["r_k"].reshape(-1))] + [cols(a[n][0]) for n in ("gn_g", "gn_b", "dw_b", "cln_g", "cln_b")]
                         + [a["dw_w"][0].reshape(TAPS, CT, P).transpose(2, 1, 0).reshape(P, -1)], axis=1)
    arr = {
        "xT": xT, "const": constants(), "vec": vec,
        "memT": a["mem_prompt"][0].T.reshape(KT, P, MEM).transpose(1, 0, 2),
        "lora_wa": np.concatenate([a["w_decay_up"][0], a["w_iclr_up"][0]]), "lora_g": a["w_glora_up"][0],
        "shift": a["state_shift"][0].reshape(NB, RW, P).transpose(2, 1, 0),
        "conv": a["state_conv"][0].reshape(NB, TAPS - 1, CT, P).transpose(3, 2, 0, 1),
        "states": a["state_wkv"][0].reshape(NB, CT, 2, CH, CH).transpose(2, 4, 1, 0, 3).reshape(P, CT, NB, CH),
        "w_mk": halves(a["w_mk"][0]), "w_mv": halves(a["w_mv"][0]), "w_out": halves(a["w_out"][0]),
        "w_q": halves(a["w_q"][0]), "w_o": halves(a["w_o"][0]),
        "cache_k": a["cache_mem_k"][0].reshape(4, 2, MEM, KT, P).transpose(0, 4, 1, 3, 2).reshape(4, P, -1),
        "cache_v": a["cache_mem_v"][0].reshape(4, 2, 2, P, D).transpose(0, 3, 1, 2, 4).reshape(4, P, -1),
        "g_moe_row": a["g_moe"].reshape(1, D), "g_final_row": a["g_final"].reshape(1, D),
        "w_router": a["w_router"][0].reshape(KT, P, NE).transpose(1, 0, 2), "b_router": a["b_router"],
        "b_gate": a["b_moe_gate"][0], "b_up": a["b_moe_up"][0], "b_down": a["b_moe_down"][0],
        "w_gate": a["w_moe_gate"][0], "w_up": a["w_moe_up"][0], "w_down": a["w_moe_down"][0],
    }
    for n in range(6):
        arr[f"w_in{n}"] = fills[n]
    nc = bacc.Bacc("TRN2", target_bir_lowering=False, num_devices=1)
    A, feed = {}, {}
    for k, v in arr.items():
        v = np.ascontiguousarray(v)
        feed["in_" + k] = v
        A[k] = nc.dram_tensor("in_" + k, v.shape, F32, kind="ExternalInput").ap()
    A["w_in"] = [A[f"w_in{n}"] for n in range(6)]
    O = {k: nc.dram_tensor("out_" + k, s, F32, kind="ExternalOutput").ap() for k, s in dict(
        y=(P, TT, D), shift=(P, RW, 1 + NB), conv=(P, CT, 1 + NB, TAPS - 1), state_p=(P, CT, CH),
        state_s=(P, CT, NB, CH), mem_k=(P, KT, MEM), mem_v=(P, 2, D)).items()}
    build(nc, A, O)
    r = run(nc, [feed], core_ids=[0]).results[0]
    y = r["out_y"].transpose(1, 0, 2).reshape(TT * P, D)
    shift = r["out_shift"].transpose(2, 1, 0).reshape(1 + NB, RW * P)
    conv = r["out_conv"].transpose(2, 3, 1, 0).reshape(1 + NB, TAPS - 1, CT * P)
    sp = r["out_state_p"].reshape(2, CH, CT, CH).transpose(2, 0, 3, 1).reshape(1, 2 * CT, CH, CH)
    ss = r["out_state_s"].reshape(2, CH, CT, NB, CH).transpose(3, 2, 0, 4, 1).reshape(NB, 2 * CT, CH, CH)
    mk = r["out_mem_k"].transpose(2, 1, 0).reshape(1, MEM, XH, D // XH)
    mv = r["out_mem_v"].transpose(1, 0, 2).reshape(1, MEM, XH, D // XH)
    return (y[0:SEQ].reshape(1, SEQ, D), y[SEQ:TOK].reshape(NB, NT, D), shift[None, 0:1], sp[None], conv[None, 0:1],
            mk[None], mv[None], shift[None, 1:], ss[None], conv[None, 1:])
```

```python
from contextlib import ExitStack

import concourse.bass as bass
from concourse import mybir

F32 = mybir.dt.float32
I32 = mybir.dt.int32
ALU = mybir.AluOpType
ACT = mybir.ActivationFunctionType
AX = mybir.AxisListType

P = 128
D = 1024
KT = D // P
SEQ = 256
NB, NT = 8, 4
TOK = SEQ + NB * NT
TT = 3
NE, TOPK = 32, 4
CAP = 64
ROUNDS = -(-TOK // CAP)
PAIRS = NE // 2
SLOTS = 6
RW = 14
CT = 4
TAPS = 31
PEXT = 1 + SEQ + NB * (1 + NT)
EXT = TAPS - 1 + SEQ + NB * (TAPS - 1 + NT)
CH = 64
NC = 5
TW = NC * CH
MEM = 256
XH = 4
KAPPA = 0.6065306597126334
LEVELS = (2, 4, 8, 16, 32)
W_IN_ORDER = (12, 13, 4, 5, 6, 7, 14, 18, 15, 19, 16, 20, 17, 21, 0, 1, 2, 3, 8, 9, 10, 11)
VEC = dict(g_mix=0, g_mem=8, g_x=16, g_moe=24, mu=32, w0=46, a0=50, k_k=54, k_a=58, r_k=62, gn_g=66, gn_b=70,
           dw_b=74, cln_g=78, cln_b=82, dw_w=86)
VECW = 86 + CT * TAPS
CONST = dict(ident=(0, 128), ones=(128, 128), before=(256, 128), mean64=(384, 128), iota=(512, 64), istack=(576, 64),
             causal=(640, 128), causal_s=(768, 128), levels=(896, 6 * 64), of_sample=(1280, 8), not_sample=(1288, 8),
             valid=(1296, 3))
CONSTW = 1300
FRONT = ([("w_in", n, n % 2) for n in range(6)] + [("w_mk", n, n) for n in range(2)] + [("w_mv", n, n) for n in range(2)]
         + [("w_out", n, n) for n in range(2)] + [("w_q", n, 2 + n) for n in range(2)]
         + [("cache_k", n, (4 + n) % 6) for n in range(4)] + [("cache_v", n, 2 + n) for n in range(4)]
         + [("w_o", n, n) for n in range(2)])
FIRST_SLOT = 2
FRONT_FILLS = [sum(f[2] == i for f in FRONT) for i in range(SLOTS)]


def front_fill(name, part):
    at = [f[:2] for f in FRONT].index((name, part))
    slot = FRONT[at][2]
    return slot, sum(f[2] == slot for f in FRONT[:at])

def build(nc, A, O):
    with ExitStack() as ctx:
        def sb(name, shape, dt=F32):
            return ctx.enter_context(nc.sbuf_tensor(name, shape, dt))

        def sem(name):
            return ctx.enter_context(nc.semaphore(name))

        def part(base, at, *dims):
            n = 1
            for d in dims:
                n *= d
            a = base[:, at:at + n]
            names = "abcd"[:len(dims)]
            if len(dims) == 1:
                return a
            return a.rearrange(f"p ({' '.join(names)}) -> p {' '.join(names)}", **dict(zip(names, dims)))

        SLOT = 4 * D
        ring = sb("ring", [P, SLOTS * SLOT])
        scratch = ring[:, 2 * SLOT:]
        arena = sb("arena", [P, 23224])
        xT = sb("xT", [P, KT, TT * P])
        const = sb("const", [P, CONSTW])
        vec = sb("vec", [P, VECW])
        slot = [part(ring, i * SLOT, KT, 512) for i in range(SLOTS)]

        def C(name):
            at, n = CONST[name]
            return const[:, at:at + n]

        def V(name, c=0):
            return vec[:, VEC[name] + c:VEC[name] + c + 1]

        ident, ones, mean64, istack = C("ident"), C("ones"), C("mean64"), C("istack")

        eps = sb("eps", [P, 2])
        rs = sb("rs", [P, TOK])
        PC = sb("PC", [P, CT, NC - 1])
        PCs = sb("PCs", [P, CT, NB])
        shift_out = sb("shift_out", [P, RW, 1 + NB])
        amax = sb("amax", [P, 9])
        asum = sb("asum", [P, 9])
        hT = part(arena, 0, KT, TOK)
        memT = part(arena, 2304, KT, MEM)
        QBp = part(arena, 0, NC - 1, CT, P)
        memK = part(arena, 4352, KT, MEM)
        memV = part(arena, 6400, 2, D)
        mix = part(arena, 8448, KT, TOK)
        ext = part(arena, 10752, CT, EXT)
        kk = part(arena, 12984, CT, TW)
        kmod = part(arena, 14264, CT, TW)
        tmp = part(arena, 15544, CT, TW)
        tmp2 = part(arena, 16824, CT, TW)
        QK = part(arena, 12984, NC, CT, 3 * CH)
        Vtok = part(arena, 16824, NC, CT, CH)
        gate = part(arena, 18104, CT, TW)
        QR = part(arena, 19384, CT, NC, 3 * CH)
        lora_wa = part(arena, 19384, 512)
        lora_g = part(arena, 19384 + 512, 512)
        shift_in = part(arena, 19384 + 1024, RW, NB)
        tlora = part(arena, 19384 + 1152, 2, TW)
        q = part(arena, 19384, KT, TOK)
        xsq = part(arena, 12984, KT, TOK)
        probs = part(arena, 12984, 8, MEM)
        probsT = part(arena, 15032, 2, 8, P)
        osam = part(arena, 17080, MEM)
        ssam = part(arena, 10752, NB, MEM)
        ssamT = part(arena, 2304, 2 * NB, P)
        rs_mem = tmp2[:, 0, 0:MEM]
        x_tok = part(arena, 0, TT, D)
        h_tok = part(arena, 3072, TT, D)
        gf_row = arena[:, 7168:8192]
        xe = part(arena, 8448, KT, 2, CAP)
        gmin = arena[:, 9472:9984]
        sig = arena[:, 9984:10496]
        b_gate = arena[0:NE, 10752:11776]
        b_up = arena[0:NE, 11776:12800]
        b_down = arena[0:NE, 12800:13824]
        ug = arena[:, 14336:14848]
        hid = arena[:, 14848:15360]
        hexT = part(arena, 15360, 4, 2, CAP)
        ye = (arena[:, 15872:16384], arena[:, 13824:14336])
        gT = part(arena, 16384, 2, TT * P)
        pick = part(arena, 17152, TT, 2, CAP)
        wpick = part(arena, 17536, TT, 2, 2, CAP)
        combT = arena[0:NE, 18304:18688]
        one_e = part(arena, 18688, 2, CAP)[0:NE]
        w_r = part(arena, 18816, KT, NE)
        b_r = arena[:, 19072:19104]
        logit = part(arena, 19104, TT, NE)
        top8 = part(arena, 19200, TT, 8)
        over = part(arena, 19224, TT, NE)
        tie = part(arena, 19320, TT, NE)
        tiecum = part(arena, 19416, TT, NE)
        mask = part(arena, 19512, TT, NE)
        comb = part(arena, 19608, TT, NE + 2)
        pos = part(arena, 19710, TT, NE + 2)
        zero = arena[:, 19812:19844]
        need = arena[:, 19844:19847]
        esum = arena[:, 19847:19850]
        ntop = arena[:, 19850:19853]
        ssq = arena[:, 19853:19856]
        sqx = part(arena, 20152, KT, TT * P)
        rstd = ssq
        load = arena[:, 19856:19857]
        load_i = sb("load_i", [P, 1], I32)
        y = x_tok
        g_moe = vec[:, VEC["g_moe"]:VEC["g_moe"] + KT]
        before, iota, valid = C("before"), C("iota"), C("valid")
        pext = part(scratch, 0, RW, PEXT)
        z = part(scratch, 4160, RW, TW)
        sw = part(scratch, 8640, CT, TW)
        cum = part(scratch, 9920, CT, TW)
        Pm = part(scratch, 11200, CT, TW)
        Pinv = part(scratch, 12480, CT, TW)
        Pex = part(scratch, 13760, CT, TW)
        rmask = Pex
        iclr = part(scratch, 15040, CT, TW)
        bt = part(scratch, 0, CT, TW)
        kt = part(scratch, 1280, CT, TW)
        QS = part(scratch, 1280, CT, CH)
        S0s = part(scratch, 5120, CT, NB, CH)
        LT = part(scratch, 2560, NC, CT, P)
        X = part(scratch, 5120, NC, CT, P)
        XT = part(scratch, 7680, NC, CT, P)
        Zs = part(scratch, 10240, NC, CT, P)
        Mk = part(scratch, 12800, 2, CT, P)
        yT = part(scratch, 13824, CT, TW)
        Wsb = part(scratch, 15104, CT, CH)
        Usb = part(scratch, 15360, CT, CH)
        Ssb = part(scratch, 15616, CT, CH)
        S0T = part(scratch, 15872, CT, CH)
        WY = part(scratch, 16128, CT, CH)
        Um = part(scratch, 2560, CT, NB, CH)
        Vm = part(scratch, 7680, CT, NB, CH)
        Wf = part(scratch, 10240, CT, NB, CH)
        t1 = part(scratch, 10240, CT, TW)
        t2 = part(scratch, 11520, CT, TW)
        tsq = part(scratch, 2560, CT, TW)

        def QB(n):
            return QBp[:, n, :, :] if n < NC - 1 else bt[:, :, 0:P]

        ps = ctx.enter_context(nc.psum_tensor("ps", [P, 8, 512], F32))

        psX = ps[:, 0:2, :].rearrange("p b f -> p (b f)")
        psY = ps[:, 2:4, :].rearrange("p b f -> p (b f)")
        psG, psU, psD, psT = (ps[:, b, :] for b in (4, 5, 6, 7))
        psP = [psX, psY]

        INV = NC + (len(LEVELS) - 1) * (NC - 1)
        NAMES = """x_in2 router_in wr_ready xsq down_done sum_ps x_in const_in mem_in lora_in shift_ld ext_ld state_ld sq_done log root kk_max h_done mem_h
            pool_i p_ps p_out z_done convgate u_done tl lora_ps sw_done a_done g_done kk_done scan cumex exps pc_done
            mk_ps mk_out mv_ps mv_out prep mix_b v_ps v_out cm_ps cm_out tok_ps tok_out lt_copied x0t x0_ps x0_out
            m_ready z_ps z_out xz_ps x_add xt_ps xt_out ws_ps ws_out u_ps u_out ys_ps s_out y_out st_ps s0_out
            sf_ps wf um_ready sd_ps snew yc cc cnorm csig mix_done
            conv wout_ps xres q_ps q_out s_ps s_max s_exp s_norm pt_ps pt_out o_ps o_out
            sk_ps ss_max ss_exp ss_norm st2_ps st2_out sv_ps so_out so_ps oT_out wo_ps xres2 osent conv_sent state_sent dve_c
            small_in xt_done ssq_done logit_ps max_done exp_done mask_done pos_ps
            route_ready 
            pick_ready disp_done xe_ready one_ready gate_done g_ready sig_ready up_done wpickT_done gT_ready hid_ready hT_done hT_ready
            ye_ready scat_done y_added fin_ssq out_ready out_sent round_pos pool_c dve_m""".split()
        S = {n: sem(n) for n in NAMES}
        slot_in = [sem(f"slot_in{i}") for i in range(SLOTS)]
        slot_free = [sem(f"slot_free{i}") for i in range(SLOTS)]
        block = ctx.enter_context(nc.Block())

        def counted(eng):
            n = {}

            def tell(name, ins, wait=True):
                ins.then_inc(S[name], 1)
                n[name] = n.get(name, 0) + 1
                if wait:
                    eng.wait_ge(S[name], n[name])
            return tell

        class Chain:
            def __init__(self, eng, s, base=0):
                self.eng, self.s, self.base, self.n = eng, s, base, 0

            def __call__(self, ins):
                ins.then_inc(self.s, 1)
                self.n += 1
                self.eng.wait_ge(self.s, self.base + self.n)

        @block.sync
        def _(sp):
            sp.dma_start(xT[:, 0:4, :], A["xT"][:, 0:4, :]).then_inc(S["x_in"], 16)
            sp.dma_start(xT[:, 4:, :], A["xT"][:, 4:, :]).then_inc(S["x_in2"], 16)
            sp.dma_start(const[:, :], A["const"]).then_inc(S["const_in"], 16)
            sp.dma_start(vec[:, :], A["vec"]).then_inc(S["const_in"], 16)

            def fill(name, n, *waits):
                i, _ = front_fill(name, n)
                for s, v in waits:
                    sp.wait_ge(S[s], v)
                src = A[name][n]
                dst = part(ring, i * SLOT, src.shape[1])
                sp.dma_start(dst, src).then_inc(slot_in[i], 16)

            fill("w_in", 0)
            sp.dma_start(memT, A["memT"]).then_inc(S["mem_in"], 16)
            sp.dma_start(shift_in, A["shift"]).then_inc(S["shift_ld"], 16)
            fill("w_in", 1)
            sp.dma_start(lora_wa, A["lora_wa"]).then_inc(S["lora_in"], 16)
            sp.dma_start(lora_g, A["lora_g"]).then_inc(S["lora_in"], 16)
            for c in range(CT):
                sp.dma_start(ext[:, c, TAPS - 1 + SEQ:].rearrange("p (b t) -> p b t", b=NB)[:, :, 0:TAPS - 1],
                             A["conv"][:, c, :, :]).then_inc(S["ext_ld"], 16)
            for n in range(2, 6):
                fill("w_in", n, ("p_ps", 4 * (n - 1)))
            fill("w_mk", 0, ("p_ps", 20))
            fill("w_mk", 1, ("p_ps", 22))
            fill("w_mv", 0, ("mk_ps", 4))
            sp.wait_ge(S["z_ps"], INV)
            sp.dma_start(S0s, A["states"]).then_inc(S["state_ld"], 16)
            fill("w_mv", 1, ("mk_ps", 8))
            fill("w_out", 0, ("mv_ps", 2))
            fill("w_out", 1, ("mv_ps", 4))
            sp.wait_ge(S["mix_done"], 2)
            sp.dma_start(w_r, A["w_router"]).then_inc(S["router_in"], 16)
            sp.dma_start(b_r, A["b_router"].broadcast_to([P, NE])).then_inc(S["router_in"], 16)
            fill("w_q", 0)
            fill("w_q", 1, ("osent", 16 * 3))
            fill("cache_k", 0)
            sp.wait_ge(S["state_sent"], 16)
            fill("cache_k", 1)
            fill("cache_k", 2, ("wout_ps", 4))
            fill("cache_k", 3, ("wout_ps", 8))
            fill("cache_v", 0, ("q_ps", 4))
            fill("cache_v", 1, ("q_ps", 8))
            fill("cache_v", 2, ("sk_ps", 1))
            fill("cache_v", 3, ("sk_ps", 2))
            fill("w_o", 0, ("sk_ps", 3))
            fill("w_o", 1, ("sk_ps", 4))
            sp.wait_ge(S["oT_out"], 1)
            sp.wait_ge(S["o_out"], 1)
            sp.dma_start(gf_row, A["g_final_row"].broadcast_to([P, D])).then_inc(S["small_in"], 16)
            for dst, name in ((b_gate, "b_gate"), (b_up, "b_up"), (b_down, "b_down")):
                sp.dma_start(dst, A[name]).then_inc(S["small_in"], 16)
            MATRICES = ((A["w_gate"], 0), (A["w_up"], 0), (A["w_gate"], 1), (A["w_up"], 1), (A["w_down"], 0), (A["w_down"], 1))
            last_front = [("wo_ps", 4), ("wo_ps", 8)] + [("sv_ps", n + 1) for n in range(4)]

            def experts(q, s, first):
                for n, (w, p) in enumerate(MATRICES):
                    for c in range(2):
                        i = (FIRST_SLOT + 2 * n + c) % SLOTS
                        if first and n < 3:
                            sem_, val = last_front[i]
                            sp.wait_ge(S[sem_], val)
                        else:
                            sp.wait_ge(slot_free[i], 2 * s + n // 3)
                        src = w[bass.ds(2 * q + p, 1), c * 512:(c + 1) * 512, :]
                        sp.dma_start(part(ring, i * SLOT, 4, D), src.rearrange("a (k p) f -> p (a k) f", p=P)).then_inc(slot_in[i], 16)

            experts(0, 0, True)
            with sp.Fori(1, PAIRS) as q:
                experts(q, q, False)
            sp.wait_ge(S["route_ready"], 1)
            n = sp.value_load(load_i[0:1, 0:1], min_val=0, max_val=TOK)
            with sp.Fori(1, ROUNDS) as r:
                with sp.If(n > r * CAP):
                    with sp.Fori(0, PAIRS) as q:
                        experts(q, r * PAIRS + q, False)
            for j in range(TT):
                sp.wait_ge(S["out_ready"], j + 1)
                sp.dma_start(O["y"][:, j, :], h_tok[:, j, :]).then_inc(S["out_sent"], 16)
            sp.wait_ge(S["out_sent"], 16 * TT)
            sp.wait_ge(S["osent"], 16 * 3)
            sp.wait_ge(S["conv_sent"], 16 * 9)
            sp.wait_ge(S["state_sent"], 16)

        def rounds(eng, n, step_fn, before_round=None):
            with eng.Fori(0, ROUNDS) as r:
                with eng.If(n > r * CAP):
                    if before_round:
                        before_round(r)
                    with eng.Fori(0, PAIRS) as q:
                        step_fn(r, q, r * PAIRS + q)

        @block.gpsimd
        def _(pool):
            g = nc.gpsimd
            tell = counted(pool)
            tell("pool_i", g.memset(eps[:, 0:1], 1e-5), False)
            tell("pool_i", g.memset(eps[:, 1:2], 64e-5), False)
            tell("pool_i", g.memset(pext[:, :, 0:1], 0.0), False)
            tell("pool_i", g.memset(z[:, :, TOK:TW], 0.0), False)
            tell("pool_i", g.memset(ext[:, :, 0:TAPS - 1], 0.0), False)
            tell("pool_i", g.memset(rmask, 1.0))
            tell("pool_i", g.memset(rmask[:, :, 0:SEQ].rearrange("p c (n t) -> p c n t", t=CH)[:, :, :, 0:1], 0.0), False)
            tell("pool_i", g.memset(rmask[:, :, SEQ:TW].rearrange("p c (n t) -> p c n t", t=NT)[:, :, :, 0:1], 0.0), False)
            pool.wait_ge(S["shift_ld"], 16)
            tell("pool_i", g.tensor_copy(pext[:, :, 1 + SEQ:].rearrange("p c (b t) -> p c b t", b=NB)[:, :, :, 0:1],
                                         shift_in.unsqueeze(3)))

            pool.wait_ge(S["p_out"], 2 * RW)
            tell("pool_i", g.tensor_copy(shift_out[:, :, 0:1], pext[:, :, SEQ:SEQ + 1]), False)
            tell("pool_i", g.tensor_copy(shift_out[:, :, 1:].unsqueeze(3),
                                         pext[:, :, 1 + SEQ:].rearrange("p c (b t) -> p c b t", b=NB)[:, :, :, NT:NT + 1]))
            pool.dma_start(O["shift"], shift_out[:, :, :]).then_inc(S["conv_sent"], 16)
            pool.wait_ge(S["exps"], 1)
            tell("pc_done", g.tensor_copy(PC[:, :, :].unsqueeze(3),
                                          Pm.rearrange("p c (n t) -> p c n t", t=CH)[:, :, 0:NC - 1, CH - 1:CH]), False)
            tell("pc_done", g.tensor_copy(PCs[:, :, :].unsqueeze(3),
                                          Pm[:, :, SEQ:TOK].rearrange("p c (n t) -> p c n t", t=NT)[:, :, :, NT - 1:NT]))
            pool.wait_ge(S["u_done"], 2 * CT)
            for c in range(CT):
                pool.dma_start(O["conv"][:, c, 0, :], ext[:, c, SEQ:SEQ + TAPS - 1]).then_inc(S["conv_sent"], 16)
                pool.dma_start(O["conv"][:, c, 1:, :],
                               ext[:, c, TAPS - 1 + SEQ:].rearrange("p (b t) -> p b t", b=NB)[:, :, NT:]).then_inc(S["conv_sent"], 16)
            pool.wait_ge(S["prep"], 1)
            tell("lt_copied", g.tensor_copy(QR.rearrange("p c n t -> p (c n) t")[:, :, 2 * CH:],
                                            istack.unsqueeze(1).broadcast_to([P, CT * NC, CH])), False)
            tell("lt_copied", g.memset(LT, 0.0), False)
            tell("lt_copied", g.memset(S0T, 0.0), False)
            pool.wait_ge(S["tok_ps"], NC)
            tell("lt_copied", g.tensor_copy(QS.rearrange("p c (a t) -> p c a t", a=2),
                                            QR[:, :, NC - 1, 0:2 * CH].rearrange("p c (a t) -> p c a t", a=2)[:, :, :, 0:NB * NT]))
            pool.wait_ge(S["mk_out"], 8)
            pool.dma_start(O["mem_k"], memK).then_inc(S["osent"], 16)
            pool.wait_ge(S["s0_out"], NC - 1)
            pool.dma_start(O["state_p"], S0T).then_inc(S["state_sent"], 16)
            pool.wait_ge(S["mv_out"], 4)
            pool.dma_start(O["mem_v"], memV).then_inc(S["osent"], 16)
            pool.wait_ge(S["snew"], 2)
            pool.dma_start(O["state_s"], S0s).then_inc(S["osent"], 16)
            pool.wait_ge(S["xres2"], 1)
            g.memset(zero, 1.0)
            g.memset(pos[:, :, NE:NE + 2], -1.0)
            tell("pool_c", g.memset(comb[:, :, NE:NE + 2], 0.0), False)
    
        @block.tensor
        def _(pe):
            readers = {}

            def take(*banks):
                for b in banks:
                    for s, v in readers.pop(b, []):
                        pe.wait_ge(S[s], v)

            def mm(out, lhsT, rhs, start=True, stop=True):
                return nc.tensor.matmul(out, lhsT, rhs, start=start, stop=stop)

            def linear(name, n, src, width, banks, done, first, reader, tiles=4, steps=None, after=None):
                i, f = front_fill(name, n)
                pe.wait_ge(slot_in[i], 16 * (f + 1))
                for m in range(tiles):
                    b = banks[(first + m) % len(banks)]
                    take(b)
                    w = part(ring, i * SLOT, KT, 128 * tiles)
                    for k in range(KT):
                        if steps and n == 0 and m == 0:
                            pe.wait_ge(S[steps[0]], steps[1] + k)
                        last = mm(ps[:, b, 0:width], w[:, k, m * P:(m + 1) * P], src[:, k, 0:width], k == 0, k == KT - 1)
                    last.then_inc(S[done], 1)
                    readers[b] = [reader(first + m)]
                    if after:
                        after(first + m)

            pe.wait_ge(S["const_in"], 32)
            def squares(n, src, w, bank):
                pe.wait_ge(S["sq_done"], n)
                take(bank)
                for k in range(KT):
                    last = mm(ps[:, bank, 0:w], ones, src[:, k, :], k == 0, k == KT - 1)
                last.then_inc(S["sum_ps"], 1)
                readers[bank] = [("root", n)]

            squares(1, mix, TOK, 0)

            def p_reader(i):
                if W_IN_ORDER[i] < RW:
                    return "p_out", 2 * sum(c < RW for c in W_IN_ORDER[:i + 1])
                return "u_done", 2 * ((W_IN_ORDER[i] - RW) % CT + 1)

            for n in range(6):
                linear("w_in", n, hT, TOK, range(8), "p_ps", 4 * n, p_reader, 4 if n < 5 else 2, steps=("h_done", 1))
                if n == 0:
                    squares(2, part(arena, 4352, KT, MEM), MEM, 7)
            pe.wait_ge(S["lora_in"], 32)
            pe.wait_ge(S["tl"], 2)
            for c in range(CT):
                take(c)
                mm(ps[:, c, 0:TW], lora_wa[0:64, c * P:(c + 1) * P], tlora[0:64, 0, :]).then_inc(S["lora_ps"], 1)
            for c in range(CT):
                take(4 + c)
                mm(ps[:, 4 + c, 0:TW], lora_wa[64:P, c * P:(c + 1) * P], z[64:P, 12, :]).then_inc(S["lora_ps"], 1)
            for c in range(CT):
                pe.wait_ge(S["sw_done"], c + 1)
                mm(ps[:, c, 0:TW], lora_g[:, c * P:(c + 1) * P], tlora[:, 1, :]).then_inc(S["lora_ps"], 1)
                readers[c] = [("g_done", c + 1)]
                readers[4 + c] = [("a_done", c + 1)]
            pe.wait_ge(S["sq_done"], 3)
            for c in range(CT):
                take(4 + c)
                last = mm(ps[:, 4 + c, 0:TW], mean64, tmp[:, c, :])
                readers[4 + c] = [("kk_max", 1)]
            last.then_inc(S["sum_ps"], 1)
            def mem_piece(i):
                if i < 16:
                    m, first, steps = i // 2, 4 * (i % 2), 4
                    b = m % 4 if m < 6 else m - 2
                    slot_i, f = front_fill("w_mk", m // 4)
                    w = part(ring, slot_i * SLOT, KT, 512)[:, :, m % 4 * P:(m % 4 + 1) * P]
                    out, done, reader = ps[:, b, 0:MEM], "mk_ps", ("mk_out", m + 1)
                else:
                    m, first, steps = (i - 16) // 4, 2 * (i % 4), 2
                    b = 4 + (m + 2) % 4
                    slot_i, f = front_fill("w_mv", m // 2)
                    out, done, reader = ps[:, b, :], "mv_ps", ("mv_out", m + 1)
                if first == 0:
                    pe.wait_ge(slot_in[slot_i], 16 * (f + 1))
                    take(b)
                for k in range(first, first + steps):
                    if i < 16:
                        last = mm(out, w[:, k, :], memT[:, k, :], k == 0, k == KT - 1)
                    else:
                        last = mm(out, memT[:, k, m % 2 * P:(m % 2 + 1) * P], slot[slot_i][:, k, :], k == 0, k == KT - 1)
                if first + steps == KT:
                    last.then_inc(S[done], 1)
                    readers[b] = [reader]

            pe.wait_ge(S["mem_h"], KT)
            for i in range(12):
                mem_piece(i)
            pe.wait_ge(S["prep"], 1)
            take(4, 5, 6, 7)
            for c in range(CT):
                last = mm(ps[:, 4 + c, 0:TW], mean64, tmp[:, c, :])
                readers[4 + c] = [("mix_b", 1)]
            last.then_inc(S["sum_ps"], 1)
            H = [slice(0, CH), slice(CH, P)]
            take(4, 5, 6)
            for n in range(NC):
                for c in range(CT):
                    for o in H:
                        last = mm(ps[o, 4 + n // 2, (n % 2) * 256 + c * CH:(n % 2) * 256 + (c + 1) * CH],
                                  z[o, 8 + c, n * CH:(n + 1) * CH], ident[o, o])
            last.then_inc(S["v_ps"], 1)
            for b in (4, 5, 6):
                readers[b] = [("v_out", 1)]
            pe.wait_ge(S["lt_copied"], 1)
            for n in range(NC):
                for w, src in enumerate((bt, kt)):
                    b = 2 * (n % 2) + w
                    take(b)
                    for c in range(CT):
                        for o in H:
                            last = mm(ps[o, b, c * P:(c + 1) * P], src[o, c, n * CH:(n + 1) * CH], QR[o, c, n, 0:P])
                    last.then_inc(S["cm_ps"], 1)
                    readers[b] = [("cm_out", 2 * n + w + 1)]
                b = 4 + n % 2
                take(b)
                for w, src in enumerate((bt, kt)):
                    for c in range(CT):
                        for o in H:
                            last = mm(ps[o, b, w * 256 + c * CH:w * 256 + (c + 1) * CH], src[o, c, n * CH:(n + 1) * CH], ident[o, o])
                last.then_inc(S["tok_ps"], 1)
                readers[b] = [("tok_out", n + 1)]
            for n in range(NC):
                b = 6 + n % 2
                pe.wait_ge(S["x0t"], n + 1)
                take(b)
                for c in range(CT):
                    last = nc.tensor.transpose(ps[:, b, c * P:(c + 1) * P], XT[:, n, c, :], ident)
                last.then_inc(S["x0_ps"], 1)
                readers[b] = [("x0_out", n + 1)]
            nb = 0
            for l, _ in enumerate(LEVELS):
                ns = NC if l == 0 else NC - 1
                g0 = 0 if l == 0 else NC + (l - 1) * (NC - 1)
                if l == 0:
                    pe.wait_ge(S["x0_out"], NC)
                for n in range(ns):
                    b = nb % 8
                    nb += 1
                    take(b)
                    pe.wait_ge(S["m_ready"], g0 + n + 1)
                    for c in range(CT):
                        last = mm(ps[:, b, c * P:(c + 1) * P], Mk[:, (g0 + n) % 2, c, :], X[:, n, c, :])
                    last.then_inc(S["z_ps"], 1)
                    readers[b] = [("z_out", g0 + n + 1)]
                for n in range(ns):
                    b = nb % 8
                    nb += 1
                    take(b)
                    pe.wait_ge(S["z_out"], g0 + n + 1)
                    if l > 0:
                        pe.wait_ge(S["xt_out"], (0 if l == 1 else NC + (l - 2) * (NC - 1)) + n + 1)
                    for c in range(CT):
                        if l < len(LEVELS) - 1:
                            last = mm(ps[:, b, c * P:(c + 1) * P], XT[:, n, c, :], Zs[:, n, c, :])
                        else:
                            last = mm(ps[:, b, c * P:(c + 1) * P], Zs[:, n, c, :], XT[:, n, c, :])
                    last.then_inc(S["xz_ps"], 1)
                    readers[b] = [("x_add", g0 + n + 1)]
                if l < len(LEVELS) - 1:
                    for n in range(ns):
                        b = nb % 8
                        nb += 1
                        take(b)
                        pe.wait_ge(S["x_add"], g0 + n + 1)
                        for c in range(CT):
                            last = nc.tensor.transpose(ps[:, b, c * P:(c + 1) * P], X[:, n, c, :], ident)
                        last.then_inc(S["xt_ps"], 1)
                        readers[b] = [("xt_out", g0 + n + 1)]
            pe.wait_ge(S["x_add"], INV)
            pe.wait_ge(S["tok_out"], NC)
            pe.wait_ge(S["cm_out"], 2 * NC)
            take(*range(8))

            def heads(*fs):
                for c in range(CT):
                    for i, f in enumerate(fs):
                        for h, o in enumerate(H):
                            last = f(c, h, o, i == 0, i == len(fs) - 1)
                return last

            for n in range(NC - 1):
                pe.wait_ge(S["s0_out"], n) if n else pe.wait_ge(S["lt_copied"], 3)

                W, Y = (lambda o, c: ps[o, 0, c * CH:(c + 1) * CH]), (lambda o, c: ps[o, 2, c * P:(c + 1) * P])
                heads(lambda c, h, o, *at: mm(W(o, c), QK[o, n, c, 0:CH], Vtok[o, n, c, :], *at),
                      lambda c, h, o, *at: mm(W(o, c), QR[o, c, n, 0:CH], S0T[o, c, :], *at)).then_inc(S["ws_ps"], 1)
                mem_piece(12 + 5 * n)
                pe.wait_ge(S["ws_out"], n + 1)
                heads(lambda c, h, o, *at: mm(ps[o, 1, c * CH:(c + 1) * CH], XT[o, n, c, o], Wsb[o, c, :])).then_inc(S["u_ps"], 1)
                mem_piece(13 + 5 * n)
                if n:
                    pe.wait_ge(S["y_out"], n)
                pe.wait_ge(S["u_out"], n + 1)
                heads(lambda c, h, o, *at: mm(Y(o, c), S0T[o, c, :], QR[o, c, n, CH:3 * CH], *at),
                      lambda c, h, o, *at: mm(Y(o, c), Vtok[o, n, c, :], QK[o, n, c, CH:3 * CH], *at),
                      lambda c, h, o, *at: mm(Y(o, c), Usb[o, c, :], QB(n)[o, c, :], *at)).then_inc(S["ys_ps"], 1)
                mem_piece(14 + 5 * n)
                pe.wait_ge(S["s_out"], n + 1)
                heads(lambda c, h, o, *at: mm(ps[o, 3, c * CH:(c + 1) * CH], Ssb[o, c, :], ident[o, o])).then_inc(S["st_ps"], 1)
                mem_piece(15 + 5 * n)
                mem_piece(16 + 5 * n)
            pe.wait_ge(S["state_ld"], 16)
            pe.wait_ge(S["lt_copied"], 4)
            take(4, 5, 6, 7)
            R = [slice(0, NB * NT), slice(CH, CH + NB * NT)]
            for c in range(CT):
                for o in H:
                    last = mm(ps[o, 4 + c, :], QS[o, c, :],
                              S0s[o, c, :, :].rearrange("p b i -> p (b i)"))
                last.then_inc(S["sf_ps"], 1)
            n = NC - 1
            pe.wait_ge(S["s0_out"], NC - 1)
            heads(lambda c, h, o, *at: mm(ps[o, 0, c * CH:(c + 1) * CH], QK[o, n, c, 0:CH], Vtok[o, n, c, :])).then_inc(S["ws_ps"], 1)
            pe.wait_ge(S["ws_out"], NC)
            heads(lambda c, h, o, *at: mm(ps[o, 1, c * CH:(c + 1) * CH], XT[o, n, c, o], Wsb[o, c, :])).then_inc(S["u_ps"], 1)
            pe.wait_ge(S["u_out"], NC)
            pe.wait_ge(S["y_out"], NC - 1)

            heads(lambda c, h, o, *at: mm(ps[o, 2, c * 32:(c + 1) * 32], Vtok[R[h], n, c, :], QK[R[h], n, c, CH:CH + 32], *at),
                  lambda c, h, o, *at: mm(ps[o, 2, c * 32:(c + 1) * 32], Usb[R[h], c, :], QB(n)[R[h], c, 0:32], *at))
            for c in range(CT):
                for h, o in enumerate(H):
                    r = slice(CH * h + 32, CH * h + 64)
                    last = mm(ps[o, 3, c * 32:(c + 1) * 32], WY[r, c, :], ident[r, r])
            last.then_inc(S["ys_ps"], 1)
            pe.wait_ge(S["conv"], CT * TAPS)
            for c in range(CT):
                last = mm(ps[:, 1, 0:TOK], ones, mix[:, CT + c, :], c == 0, c == CT - 1)
            last.then_inc(S["sum_ps"], 1)
            pe.wait_ge(S["um_ready"], 2)
            pe.wait_ge(S["wf"], CT)
            heads(lambda c, h, o, *at: mm(ps[o, 4 + c, :], QB(n)[R[h], c, CH:], Um[R[h], c, :, :].rearrange("p b i -> p (b i)"), *at),
                  lambda c, h, o, *at: mm(ps[o, 4 + c, :], QK[R[h], n, c, 2 * CH:], Vm[R[h], c, :, :].rearrange("p b i -> p (b i)"),
                                          *at)).then_inc(S["sd_ps"], 1)
            pe.wait_ge(S["sq_done"], 4)
            for c in range(CT):
                last = mm(ps[:, 0, 0:TOK], ones, t1[:, c, 0:TOK], c == 0, c == CT - 1)
            last.then_inc(S["sum_ps"], 1)
            pe.wait_ge(S["y_out"], NC)
            pe.wait_ge(S["cc"], 1)
            for c in (1, 2, 3, 0):
                if c == 0:
                    pe.wait_ge(S["root"], 4)
                last = mm(ps[:, c, 0:TOK], mean64, yT[:, c, 0:TOK])
            last.then_inc(S["sum_ps"], 1)
            pe.wait_ge(S["snew"], 1)
            pe.wait_ge(S["sq_done"], 5)
            for c in range(CT):
                last = mm(ps[:, 4 + c, 0:TOK], mean64, tsq[:, c, 0:TOK])
            last.then_inc(S["sum_ps"], 1)
            for part_, ks in enumerate((range(CT, KT), range(CT))):
                pe.wait_ge(S["mix_done"], part_ + 1)
                for m in range(KT):
                    if m == 4 and not part_:
                        pe.wait_ge(S["root"], 5)
                    i, f = front_fill("w_out", m // 4)
                    pe.wait_ge(slot_in[i], 16 * (f + 1))
                    for k in ks:
                        last = mm(ps[:, m, 0:TOK], part(ring, i * SLOT, KT, 512)[:, k, m % 4 * P:(m % 4 + 1) * P],
                                  mix[:, k, 0:TOK], k == CT, k == CT - 1)
                    if part_:
                        last.then_inc(S["wout_ps"], 1)
            for m in range(KT):
                readers[m] = [("xres", m + 1)]
            take(0)
            for k in range(KT):
                pe.wait_ge(S["sq_done"], 6 + k)
                last = mm(ps[:, 0, 0:TOK], ones, xsq[:, k, :], k == 0, k == KT - 1)
            last.then_inc(S["sum_ps"], 1)
            readers[0] = [("root", 6)]
            for n in range(2):
                linear("w_q", n, hT, TOK, range(8), "q_ps", 4 * n, lambda m: ("q_out", m + 1), steps=("h_done", KT + 1))
            pe.wait_ge(S["q_out"], 8)
            take(*range(8))
            for u in range(8):
                h, t = u // 2, u % 2
                for k in range(2):
                    last = mm(ps[:, h, t * MEM:(t + 1) * MEM], q[:, 2 * h + k, t * P:(t + 1) * P], memK[:, 2 * h + k, :], k == 0, k == 1)
            last.then_inc(S["s_ps"], 1)
            for n in range(4):
                i, f = front_fill("cache_k", n)
                keys = part(ring, i * SLOT, 2, KT, MEM)
                pe.wait_ge(slot_in[i], 16 * (f + 1))
                for b in range(2):
                    for k in range(2):
                        for h in range(XH):
                            last = mm(ps[32 * h:32 * h + 32, 4 + n, b * MEM:(b + 1) * MEM], q[:, 2 * h + k, SEQ:TOK],
                                      keys[:, b, 2 * h + k, :], k == 0, k == 1)
                last.then_inc(S["sk_ps"], 1)
            pe.wait_ge(S["s_norm"], 1)
            for t in range(2):
                for m in range(2):
                    for h in range(XH):
                        last = nc.tensor.transpose(ps[:, 2 * m + t, h * P:(h + 1) * P], probs[:, 2 * h + t, m * P:(m + 1) * P], ident)
            last.then_inc(S["pt_ps"], 1)
            pe.wait_ge(S["pt_out"], 1)
            for h in range(XH):
                for d in range(2):
                    for m in range(2):
                        last = mm(ps[:, h, d * SEQ:(d + 1) * SEQ].rearrange("p (t a) -> p t a", t=2), memV[:, m, (2 * h + d) * P:(2 * h + d + 1) * P],
                                  probsT.rearrange("p m (t h) a -> p m h t a", t=2)[:, m, h, :, :], m == 0, m == 1)
            last.then_inc(S["o_ps"], 1)
            pe.wait_ge(S["ss_norm"], 1)
            for j in range(2 * NB):
                last = nc.tensor.transpose(ps[:, 4 + j // 4, (j % 4) * P:(j % 4 + 1) * P],
                                           ssam.rearrange("p b m -> p (b m)")[:, j * P:(j + 1) * P], ident)
            last.then_inc(S["st2_ps"], 1)
            pe.wait_ge(S["st2_out"], 1)
            for n in range(4):
                i, f = front_fill("cache_v", n)
                vals = part(ring, i * SLOT, 2, 2, D)
                pe.wait_ge(slot_in[i], 16 * (f + 1))
                for j in range(4):
                    for h in range(XH):
                        last = mm(ps[32 * h:32 * h + 32, 4, 0:MEM], ssamT[:, 4 * n + j, 32 * h:32 * h + 32],
                                  vals[:, j // 2, j % 2, h * MEM:(h + 1) * MEM], n == 0 and j == 0, n == 3 and j == 3)
                last.then_inc(S["sv_ps"], 1)
            pe.wait_ge(S["so_out"], 1)
            for d in range(2):
                last = nc.tensor.transpose(ps[:, 5, d * P:(d + 1) * P], osam[:, d * P:(d + 1) * P], ident)
            last.then_inc(S["so_ps"], 1)
            pe.wait_ge(S["o_out"], 1)
            pe.wait_ge(S["oT_out"], 1)
            pe.wait_ge(S["router_in"], 32)
            pe.wait_ge(S["wr_ready"], 1)

            def route(k):
                pe.wait_ge(S["xres2"], k + 1)
                for j in range(TT):
                    nc.tensor.matmul(psT[:, j * NE:(j + 1) * NE], xT[:, k, j * P:(j + 1) * P], w_r[:, k, :],
                                     start=(k == 0 and j == 0), stop=(k == KT - 1), skip_group_check=True)
                pe.wait_ge(S["xsq"], k + 1)
                for j in range(TT):
                    last = nc.tensor.matmul(psT[:, TT * NE + j:TT * NE + j + 1], sqx[:, k, j * P:(j + 1) * P], ones[:, 0:1],
                                            start=False, stop=(k == KT - 1), skip_group_check=True)
                return last

            for n in range(2):
                linear("w_o", n, mix, TOK, range(6), "wo_ps", 4 * n, lambda m: ("xres2", m + 1),
                       after=lambda m: route(m - 1) if m else None)
            route(KT - 1).then_inc(S["logit_ps"], 1)
            for j in range(TT):
                if j == 2:
                    pe.wait_ge(S["y_added"], 1)
                for k in range(KT):
                    last = nc.tensor.transpose(psP[j % 2][:, k * P:(k + 1) * P], xT[:, k, j * P:(j + 1) * P], ident)
                last.then_inc(S["xt_done"], 1)
            pe.wait_ge(S["mask_done"], 1)
            for j in range(TT):
                for i in range(j + 1):
                    nc.tensor.matmul(psG[:, j * NE:(j + 1) * NE], ones if i < j else before, mask[:, i, :],
                                     start=(i == 0), stop=(i == j))
            for i in range(TT):
                last = nc.tensor.matmul(psG[:, TT * NE:(TT + 1) * NE], ones, mask[:, i, :],
                                        start=(i == 0), stop=(i == TT - 1))
            last.then_inc(S["pos_ps"], 1)
            pe.wait_ge(S["small_in"], 16 * 4)
            pe.wait_ge(S["route_ready"], 1)
            n = pe.value_load(load_i[0:1, 0:1], min_val=0, max_val=TOK)

            def product(ps, lhs, slots, fill, bias, done, swap=False):
                at = [slice(CAP * (h ^ swap), CAP * (h ^ swap) + CAP) for h in range(2)]
                for k in range(KT):
                    i = (FIRST_SLOT + slots + k // 4) % SLOTS
                    if k % 4 == 0:
                        pe.wait_ge(slot_in[i], 16 * (fill + 1 + FRONT_FILLS[i]))
                    for h in range(2):
                        last = nc.tensor.matmul(ps[at[h], :], lhs(k), part(ring, i * SLOT, 4, D)[:, k % 4, h * 512:(h + 1) * 512],
                                                start=(k == 0), stop=False, skip_group_check=True)
                    if k % 4 == 3:
                        last.then_inc(slot_free[i], 1)
                for h in range(2):
                    last = nc.tensor.matmul(ps[at[h], :], bias[0], bias[1][:, h * 512:(h + 1) * 512],
                                            start=False, stop=True, skip_group_check=True)
                last.then_inc(S[done], 1)

            def step(r, q, s):
                def in_xe(p):
                    return lambda k: xe[:, k, p, :]

                def in_hT(k):
                    return hexT[:, k % 4, k // 4, :]

                def turn_hid(st):
                    pe.wait_ge(S["hid_ready"], st + 1)
                    for j in range(4):
                        last = nc.tensor.transpose(psT[:, j * P:(j + 1) * P], hid[:, j * P:(j + 1) * P], ident)
                    last.then_inc(S["hT_done"], 1)

                def scatter():
                    pe.wait_ge(S["ye_ready"], 2 * s + 2)
                    for j in range(TT):
                        if j == 2:
                            pe.wait_ge(S["y_added"], 3 * s + 4)
                        for h in range(2):
                            last = nc.tensor.matmul(psP[(j + 1) % 2][:, h * 512:(h + 1) * 512], gT[:, h, j * P:(j + 1) * P],
                                                    ye[h], start=True, stop=True)
                        last.then_inc(S["scat_done"], 1)

                pe.wait_ge(S["pick_ready"], r * (PAIRS + 1) + q + 1)
                pe.wait_ge(S["y_added"], 3 * s + 2)
                for k in range(KT):
                    for j in range(TT):
                        last = nc.tensor.matmul(psX[:, k * P:(k + 1) * P], h_tok[:, j, k * P:(k + 1) * P],
                                                pick[:, j, :, :], start=(j == 0), stop=(j == TT - 1))
                last.then_inc(S["disp_done"], 1)
                pe.wait_ge(S["y_added"], 3 * s + 3)
                for p in range(2):
                    for j in range(TT):
                        last = nc.tensor.transpose(psY[:, p * 512 + j * P:p * 512 + (j + 1) * P],
                                                   wpick[:, j, p, :, :].rearrange("t a c -> t (a c)"), ident)
                last.then_inc(S["wpickT_done"], 1)
                pe.wait_ge(S["one_ready"], s + 1)
                pe.wait_ge(S["xe_ready"], s + 1)
                product(psG, in_xe(0), 0, 2 * s, (one_e[:, 0, :], b_gate), "gate_done")
                product(psU, in_xe(0), 2, 2 * s, (one_e[:, 0, :], b_up), "up_done")
                pe.wait_ge(S["g_ready"], 2 * s + 1)
                product(psG, in_xe(1), 4, 2 * s, (one_e[:, 1, :], b_gate), "gate_done")
                turn_hid(2 * s)
                product(psU, in_xe(1), 0, 2 * s + 1, (one_e[:, 1, :], b_up), "up_done")
                pe.wait_ge(S["hT_ready"], 2 * s + 1)
                product(psD, in_hT, 2, 2 * s + 1, (one_e[:, 0, :], b_down), "down_done")
                turn_hid(2 * s + 1)
                pe.wait_ge(S["hT_ready"], 2 * s + 2)
                pe.wait_ge(S["ye_ready"], 2 * s + 1)
                product(psD, in_hT, 4, 2 * s + 1, (one_e[:, 1, :], b_down), "down_done", swap=True)
                pe.wait_ge(S["gT_ready"], s + 1)
                scatter()

            rounds(pe, n, step)

        @block.scalar
        def _(act):
            a = nc.scalar
            tell = counted(act)

            def copy(out, in_, scale=1.0):
                return a.activation(out, in_, ACT.Copy, scale=scale)

            act.wait_ge(S["x_in"], 16)
            a.activation(mix[:, 0:4, :], xT[:, 0:4, 0:TOK], ACT.Square)
            act.wait_ge(S["x_in2"], 16)
            tell("sq_done", a.activation(mix[:, 4:, :], xT[:, 4:, 0:TOK], ACT.Square), False)
            def inv_root(need, out, in_, scale, eps_at=None):
                act.wait_ge(*need)
                bias = 0.0 if eps_at is None else eps[:, eps_at:eps_at + 1]
                tell("log", a.activation(out, in_, ACT.Ln, scale=scale, bias=bias))
                tell("root", a.activation(out, out, ACT.Exp, scale=-0.5), False)

            act.wait_ge(S["pool_i"], 2)
            inv_root((S["sum_ps"], 1), rs[:, :], ps[:, 0, 0:TOK], 1.0 / D, 0)
            act.wait_ge(S["mem_in"], 16)
            tell("sq_done", a.activation(part(arena, 4352, KT, MEM), memT, ACT.Square), False)
            inv_root((S["sum_ps"], 2), rs_mem, ps[:, 7, 0:MEM], 1.0 / D, 0)
            act.wait_ge(S["pool_i"], 9)
            for i, c in enumerate(W_IN_ORDER):
                if RW <= c < RW + CT:
                    continue
                act.wait_ge(S["p_ps"], i + 1)
                if c < RW:
                    tell("p_out", copy(pext[:, c, 1:1 + SEQ], ps[:, i % 8, 0:SEQ]), False)
                    tell("p_out", copy(pext[:, c, 1 + SEQ:].rearrange("p (b t) -> p b t", b=NB)[:, :, 1:],
                                       ps[:, i % 8, SEQ:TOK].rearrange("p (b t) -> p b t", b=NB)), False)
                else:
                    j = c - RW - CT
                    if j < 2:
                        act.wait_ge(S["mem_h"], KT)
                    else:
                        act.wait_ge(S["u_done"], 2 * (j - 1))
                    tell("convgate", a.activation(tmp2[:, j % 2, 0:TOK], ps[:, i % 8, 0:TOK], ACT.Sigmoid), False)
                if i == 5:
                    act.wait_ge(S["z_done"], 1)
                    tell("tl", a.activation(tlora[0:64, 0, :], z[0:64, 12, :], ACT.Tanh), False)
                    tell("tl", a.activation(tlora[:, 1, :], z[:, 13, :], ACT.Sigmoid), False)
            for c in range(CT):
                act.wait_ge(S["lora_ps"], c + 1)
                if c == 0:
                    act.wait_ge(S["const_in"], 32)
                tell("sw_done", a.activation(sw[:, c, :], ps[:, c, 0:TW], ACT.Sigmoid, bias=V("w0", c)), False)
            for c in range(CT):
                act.wait_ge(S["lora_ps"], CT + c + 1)
                tell("a_done", a.activation(iclr[:, c, :], ps[:, 4 + c, 0:TW], ACT.Sigmoid, bias=V("a0", c)), False)
            for c in range(CT):
                act.wait_ge(S["lora_ps"], 2 * CT + c + 1)
                tell("g_done", copy(gate[:, c, :], ps[:, c, 0:TW]), False)
            act.wait_ge(S["kk_done"], 1)
            tell("sq_done", a.activation(tmp, kk, ACT.Square), False)
            inv_root((S["kk_max"], 1), tmp, tmp, 1.0)
            act.wait_ge(S["scan"], 1)
            tell("exps", a.activation(Pm, cum, ACT.Exp, scale=-KAPPA), False)
            tell("exps", a.activation(Pinv, cum, ACT.Exp, scale=KAPPA), False)
            act.wait_ge(S["cumex"], 1)
            tell("exps", a.activation(Pex, sw, ACT.Exp, scale=-KAPPA), False)

            def mem_key(m):
                act.wait_ge(S["mk_ps"], m + 1)
                tell("mk_out", copy(memK[:, m, :], ps[:, m % 4 if m < 6 else m - 2, 0:MEM]), False)

            def mem_value(m):
                act.wait_ge(S["mv_ps"], m + 1)
                tell("mv_out", copy(memV[:, m % 2, (m // 2) * 512:(m // 2 + 1) * 512], ps[:, 4 + (m + 2) % 4, :]), False)

            for m in range(6):
                mem_key(m)
            act.wait_ge(S["v_ps"], 1)
            act.wait_ge(S["mix_b"], 1)
            tell("v_out", copy(Vtok.rearrange("p n c i -> p (n c i)"), ps[:, 4:7, :].rearrange("p b f -> p (b f)")[:, 0:NC * 256]))
            for n in range(NC):
                act.wait_ge(S["tok_ps"], n + 1)
                src = ps[:, 4 + n % 2, :].rearrange("p (w c j) -> p w c j", w=2, c=CT)
                copy(QB(n)[:, :, CH:], src[:, 0, :, :])
                tell("tok_out", copy(QK[:, n, :, 2 * CH:], src[:, 1, :, :]), False)
            for n in range(NC):
                act.wait_ge(S["x0_ps"], n + 1)
                tell("x0_out", copy(X[:, n, :, :].rearrange("p c t -> p (c t)"), ps[:, 6 + n % 2, :]), False)
            nb = 0
            for l, _ in enumerate(LEVELS):
                ns = NC if l == 0 else NC - 1
                g0 = 0 if l == 0 else NC + (l - 1) * (NC - 1)
                for n in range(ns):
                    act.wait_ge(S["z_ps"], g0 + n + 1)
                    if l:
                        act.wait_ge(S["xz_ps"], (0 if l == 1 else NC + (l - 2) * (NC - 1)) + n + 1)
                    tell("z_out", copy(Zs[:, n, :, :].rearrange("p c t -> p (c t)"), ps[:, nb % 8, :]), False)
                    nb += 1
                nb += ns
                if l < len(LEVELS) - 1:
                    for n in range(ns):
                        act.wait_ge(S["xt_ps"], g0 + n + 1)
                        tell("xt_out", copy(XT[:, n, :, :].rearrange("p c t -> p (c t)"), ps[:, nb % 8, :]), False)
                        nb += 1
            for n in range(NC - 1):
                act.wait_ge(S["ws_ps"], n + 1)
                tell("ws_out", copy(Wsb.rearrange("p c i -> p (c i)"), ps[:, 0, 0:256]), False)
                if n == 0:
                    mem_key(6)
                    mem_key(7)
                else:
                    mem_value(n - 1)
                    if n == NC - 2:
                        mem_value(n)
            act.wait_ge(S["cc"], 1)
            tell("sq_done", a.activation(t1[:, :, 0:TOK], mix[:, CT:, :], ACT.Square), False)
            inv_root((S["sum_ps"], 6), rs[:, :], ps[:, 0, 0:TOK], 1.0 / (CT * P), 0)
            act.wait_ge(S["cnorm"], CT)
            tell("csig", a.activation(t1[:, :, 0:TOK], mix[:, CT:, :], ACT.Sigmoid), False)
            act.wait_ge(S["yc"], 1)
            tell("sq_done", a.activation(tsq[:, :, 0:TOK], yT[:, :, 0:TOK], ACT.Square), False)
            inv_root((S["sum_ps"], 8), t2[:, :, 0:TOK], ps[:, 4:8, 0:TOK], 1.0, 1)
            for m in range(KT):
                act.wait_ge(S["xres"], m + 1)
                tell("sq_done", a.activation(xsq[:, m, :], xT[:, m, 0:TOK], ACT.Square), False)
            inv_root((S["sum_ps"], 9), rs[:, :], ps[:, 0, 0:TOK], 1.0 / D, 0)
            for m in range(KT):
                act.wait_ge(S["q_ps"], m + 1)
                tell("q_out", copy(q[:, m, :], ps[:, m, 0:TOK]), False)
            act.wait_ge(S["s_max"], 1)
            for u in range(8):
                tell("s_exp", a.activation(probs[:, u, :], ps[:, u // 2, (u % 2) * MEM:(u % 2 + 1) * MEM], ACT.Exp,
                                           scale=1.0 / 16, bias=amax[:, u:u + 1], accum_out=asum[:, u:u + 1]), False)
            act.wait_ge(S["pt_ps"], 1)
            tell("pt_out", copy(probsT.rearrange("p m u a -> p (m u a)"), ps[:, 0:4, :].rearrange("p b f -> p (b f)")), False)
            act.wait_ge(S["ss_max"], 1)
            tell("ss_exp", a.activation(ssam, ssam, ACT.Exp, scale=1.0 / 16, bias=amax[:, 8:9], accum_out=asum[:, 8:9]), False)
            act.wait_ge(S["o_ps"], 1)
            tell("o_out", copy(mix[:, :, 0:SEQ], ps[:, 0:4, :].rearrange("p h (d t) -> p (h d) t", d=2)), False)
            act.wait_ge(S["st2_ps"], 1)
            tell("st2_out", copy(ssamT.rearrange("p j a -> p (j a)"), ps[:, 4:8, :].rearrange("p b f -> p (b f)")), False)
            act.wait_ge(S["sv_ps"], 4)
            tell("so_out", copy(osam, ps[:, 4, 0:MEM]), False)
            act.wait_ge(S["so_ps"], 1)
            for d in range(2):
                last = copy(mix.rearrange("p (h d) t -> p h d t", d=2)[:, :, d, SEQ:TOK],
                            ps[:, 5, d * P:(d + 1) * P].rearrange("p (h t) -> p h t", h=XH))
            tell("oT_out", last, False)
            for m in range(KT):
                act.wait_ge(S["xres2"], m + 1)
                tell("xsq", a.activation(sqx[:, m, :], xT[:, m, :], ACT.Square), False)
            inv_root((S["logit_ps"], 1), rstd, psT[:, TT * NE:TT * NE + TT], 1.0 / D, 0)
            act.wait_ge(S["root"], 7)
            for j in range(TT):
                act.wait_ge(S["xt_done"], j + 1)
                copy(x_tok[:, j, :], psP[j % 2][:, :])
                copy(h_tok[:, j, :], psP[j % 2][:, :], rstd[:, j:j + 1]).then_inc(S["y_added"], 1)
            act.wait_ge(S["max_done"], 1)
            for j in range(TT):
                nc.scalar.activation(comb[:, j, 0:NE], logit[:, j, :], ACT.Exp, bias=ntop[:, j:j + 1]).then_inc(S["exp_done"], 1)
            act.wait_ge(S["route_ready"], 1)
            n = act.value_load(load_i[0:1, 0:1], min_val=0, max_val=TOK)

            def step(r, q, s):
                act.wait_ge(S["wpickT_done"], s + 1)
                nc.scalar.activation(gT[:, :, :], psY.rearrange("p (a t) -> p a t", a=2)[:, :, 0:TT * P], ACT.Copy).then_inc(S["gT_ready"], 1)
                for p in range(2):
                    st = 2 * s + p
                    act.wait_ge(S["g_ready"], st + 1)
                    nc.scalar.activation(sig, gmin, ACT.Sigmoid, scale=1.702).then_inc(S["sig_ready"], 1)
                    act.wait_ge(S["hT_done"], st + 1)
                    nc.scalar.activation(hexT.rearrange("p a b c -> p (a b c)"), psT, ACT.Copy).then_inc(S["hT_ready"], 1)
                    act.wait_ge(S["down_done"], st + 1)
                    for h in range(2):
                        o = slice(CAP * (h ^ p), CAP * (h ^ p) + CAP)
                        last = nc.scalar.activation(ye[h][o], psD[o], ACT.Copy)
                    last.then_inc(S["ye_ready"], 1)

            rounds(act, n, step)
            act.wait_ge(S["fin_ssq"], 1)
            for j in range(TT):
                nc.scalar.activation(h_tok[:, j, :], y[:, j, :], ACT.Square,
                                     accum_out=ssq[:, j:j + 1]).then_inc(S["ssq_done"], 1)
            inv_root((S["ssq_done"], 3), ssq, ssq, 1.0 / D, 0)

        @block.vector
        def _(dve):
            v = nc.vector
            tell = counted(dve)

            def tt(out, x, y, op):
                return v.tensor_tensor(out, x, y, op)

            def stt(out, x, s, y, o0, o1):
                return v.scalar_tensor_tensor(out, x, s, y, o0, o1)

            def link(ins):
                tell("dve_c", ins)

            MUL, ADD, SUB = ALU.mult, ALU.add, ALU.subtract
            dve.wait_ge(S["const_in"], 32)
            dve.wait_ge(S["x_in"], 16)
            dve.wait_ge(S["x_in2"], 16)

            def norm(n, src, out, rs, w, g, done):
                dve.wait_ge(S["root"], n)
                for k in range(KT):
                    tell(done, stt(out[:, k, 0:w], src[:, k, 0:w], V(g, k), rs, MUL, MUL), False)

            norm(1, xT, hT, rs[:, :], TOK, "g_mix", "h_done")
            dve.wait_ge(S["h_done"], KT)
            norm(2, memT, memT, rs_mem, MEM, "g_mem", "mem_h")

            def shift(lo, hi):
                pe3 = pext[:, lo:hi, 1 + SEQ:].rearrange("p c (b t) -> p c b t", b=NB)
                tell("dve_c", tt(z[:, lo:hi, 0:SEQ], pext[:, lo:hi, 0:SEQ], pext[:, lo:hi, 1:1 + SEQ], SUB), False)
                link(tt(z[:, lo:hi, SEQ:TOK].rearrange("p c (b t) -> p c b t", b=NB), pe3[:, :, :, 0:NT], pe3[:, :, :, 1:], SUB))
                for c in range(lo, hi):
                    stt(z[:, c, 0:SEQ], z[:, c, 0:SEQ], V("mu", c), pext[:, c, 1:1 + SEQ], MUL, ADD)
                    zs = z[:, c, SEQ:TOK].rearrange("p (b t) -> p b t", b=NB)
                    last = stt(zs, zs, V("mu", c), pe3[:, c - lo, :, 1:], MUL, ADD)
                tell("z_done", last)

            dve.wait_ge(S["p_out"], 4)
            shift(12, 14)
            dve.wait_ge(S["p_out"], 12)
            shift(4, 8)
            for c in range(CT):
                last = v.tensor_scalar(kk[:, c, :], z[:, 4 + c, :], V("k_k", c), None, MUL)
            tell("kk_done", last)
            dve.wait_ge(S["ext_ld"], 64)
            for j in range(CT):
                dve.wait_ge(S["convgate"], j + 1)
                b = (W_IN_ORDER.index(RW + j)) % 8
                tell("u_done", tt(ext[:, j, TAPS - 1:TAPS - 1 + SEQ], ps[:, b, 0:SEQ], tmp2[:, j % 2, 0:SEQ], MUL), False)
                tell("u_done", tt(ext[:, j, TAPS - 1 + SEQ:].rearrange("p (b t) -> p b t", b=NB)[:, :, TAPS - 1:],
                                  ps[:, b, SEQ:TOK].rearrange("p (b t) -> p b t", b=NB),
                                  tmp2[:, j % 2, SEQ:TOK].rearrange("p (b t) -> p b t", b=NB), MUL), j == CT - 1)

            def conv(lo, hi):
                for k in range(lo, min(hi, TAPS)):
                    for c in range(CT):
                        w = V("dw_w", c * TAPS + k)
                        xp = ext[:, c, k:k + SEQ]
                        xs = ext[:, c, TAPS - 1 + SEQ:].rearrange("p (b t) -> p b t", b=NB)[:, :, k:k + NT]
                        yp = mix[:, CT + c, 0:SEQ]
                        ys = mix[:, CT + c, SEQ:TOK].rearrange("p (b t) -> p b t", b=NB)
                        if k == 0:
                            v.tensor_scalar(yp, xp, w, V("dw_b", c), MUL, ADD)
                            last = v.tensor_scalar(ys, xs, w, V("dw_b", c), MUL, ADD)
                        else:
                            dve.wait_ge(S["conv"], CT * (k - 1) + c + 1)
                            stt(yp, xp, w, yp, MUL, ADD)
                            last = stt(ys, xs, w, ys, MUL, ADD)
                        last.then_inc(S["conv"], 1)

            dve.wait_ge(S["pool_i"], 9)
            conv(0, 5)
            dve.wait_ge(S["p_out"], 20)
            shift(0, 4)
            conv(5, 10)
            dve.wait_ge(S["p_out"], 28)
            shift(8, 12)
            dve.wait_ge(S["sw_done"], CT)
            flat = "p c t -> p (c t)"
            tell("scan", v.tensor_tensor_scan(cum.rearrange(flat), rmask.rearrange(flat), sw.rearrange(flat), 0.0, MUL, ADD))
            tell("cumex", tt(sw, cum, sw, SUB))
            dve.wait_ge(S["sum_ps"], 3)
            tell("kk_max", v.tensor_scalar(tmp, ps[:, 4:8, 0:TW], 64.0, 1e-24, MUL, ALU.max), False)
            dve.wait_ge(S["a_done"], CT)
            for c in range(CT):
                last = v.tensor_scalar(kmod[:, c, :], iclr[:, c, :], 1.0, V("k_a", c), SUB, MUL)
            link(last)
            link(stt(kmod, kmod, 1.0, z[:, 4:8, :], ADD, MUL))
            dve.wait_ge(S["root"], 3)
            link(tt(kk, kk, tmp, MUL))
            dve.wait_ge(S["exps"], 3)
            QRv = QR.rearrange("p c n t -> p (c n) t")
            cn = "p c (n t) -> p (c n) t"
            dve.wait_ge(S["lora_ps"], 3 * CT)
            dve.wait_ge(S["pool_i"], 11)
            tt(iclr, kk, iclr, MUL)
            stt(QRv[:, :, 0:CH], kk.rearrange(cn, t=CH), -1.0, Pex.rearrange(cn, t=CH), MUL, MUL)
            tt(QRv[:, :, CH:P], z[:, 0:4, :].rearrange(cn, t=CH), Pm.rearrange(cn, t=CH), MUL)
            tt(kt, kmod, Pinv, MUL)
            for c in range(CT):
                last = stt(tmp[:, c, :], z[:, c, :], V("r_k", c), kmod[:, c, :], MUL, MUL)
            link(last)
            tell("prep", tt(bt, iclr, Pinv, MUL))
            conv(10, 11)
            dve.wait_ge(S["sum_ps"], 4)
            tell("mix_b", stt(mix[:, 0:CT, :], ps[:, 4:8, 0:TOK], 64.0, z[:, 8:12, 0:TOK], MUL, MUL))

            conv(11, 12)
            for n in range(NC):
                keep = C("causal" if n < NC - 1 else "causal_s").unsqueeze(1).broadcast_to([P, CT, P])
                dve.wait_ge(S["cm_ps"], 2 * n + 1)
                src = ps[:, 2 * (n % 2), :].rearrange("p (c t) -> p c t", c=CT)
                if n == 0:
                    dve.wait_ge(S["lt_copied"], 2)
                for o in (slice(0, CH), slice(CH, P)):
                    tt(LT[o, n, :, o], src[o, :, 0:CH], keep[o, :, 0:CH], MUL)
                tell("cm_out", tt(QB(n)[:, :, 0:CH], src[:, :, CH:], keep[:, :, CH:], MUL), False)
                dve.wait_ge(S["cm_ps"], 2 * n + 2)
                tell("cm_out", tt(QK[:, n, :, 0:P], ps[:, 2 * (n % 2) + 1, :].rearrange("p (c t) -> p c t", c=CT), keep, MUL), False)
                conv(12 + n, 13 + n)

            def level(l):
                return C("levels")[:, l * 64:(l + 1) * 64].unsqueeze(1).broadcast_to([P, 2 * CT, 64])

            halves = "p c (h t) -> p (c h) t"
            for n in range(NC):
                dve.wait_ge(S["cm_out"], 2 * n + 1)
                link(tt(XT[:, n, :, :].rearrange(halves, h=2), LT[:, n, :, :].rearrange(halves, h=2), level(0), MUL))
                tell("x0t", tt(XT[:, n, :, :], XT[:, n, :, :], ident.unsqueeze(1).broadcast_to([P, CT, P]), ADD), False)
            nb = 0
            for l, _ in enumerate(LEVELS):
                ns = NC if l == 0 else NC - 1
                g0 = 0 if l == 0 else NC + (l - 1) * (NC - 1)
                for n in range(ns):
                    g = g0 + n
                    if g >= 2:
                        dve.wait_ge(S["z_ps"], g - 1)
                    tell("m_ready", tt(Mk[:, g % 2, :, :].rearrange(halves, h=2), LT[:, n, :, :].rearrange(halves, h=2), level(l + 1), MUL), False)
                conv(17 + l, 18 + l)
                nb += ns
                for n in range(ns):
                    dve.wait_ge(S["xz_ps"], g0 + n + 1)
                    at = (X if l < len(LEVELS) - 1 else XT)[:, n, :, :].rearrange("p c t -> p (c t)")
                    tell("x_add", tt(at, at, ps[:, nb % 8, :], ADD), False)
                    nb += 1
                nb += ns
            dve.wait_ge(S["pc_done"], 2)
            half4 = ps[:, 2, :].rearrange("p (c t) -> p c t", c=CT)
            for n in range(NC - 1):
                dve.wait_ge(S["u_ps"], n + 1)
                tell("u_out", v.tensor_copy(Usb.rearrange("p c i -> p (c i)"), ps[:, 1, 0:256]), False)
                conv(22 + 3 * n, 23 + 3 * n)
                dve.wait_ge(S["ys_ps"], n + 1)
                tell("s_out", v.tensor_copy(Ssb, half4[:, :, CH:]), False)
                tell("y_out", v.tensor_copy(yT[:, :, n * CH:(n + 1) * CH], half4[:, :, 0:CH]), False)
                conv(23 + 3 * n, 24 + 3 * n)
                dve.wait_ge(S["st_ps"], n + 1)
                tell("s0_out", tt(S0T, ps[:, 3, 0:256].rearrange("p (c i) -> p c i", c=CT),
                                  PC[:, :, n:n + 1].broadcast_to([P, CT, CH]), MUL), False)
                conv(24 + 3 * n, 25 + 3 * n)
            own = C("of_sample").unsqueeze(2).broadcast_to([P, NB, CH])
            for c in range(CT):
                dve.wait_ge(S["sf_ps"], c + 1)
                tell("wf", tt(Wf[:, c, :, :], ps[:, 4 + c, :].rearrange("p (b i) -> p b i", b=NB), own, MUL))
            link(v.tensor_reduce(WY, Wf.rearrange("p c b i -> p c i b"), AX.X, ADD))
            dve.wait_ge(S["ws_ps"], NC)
            tt(Wsb.rearrange("p c i -> p (c i)"), ps[:, 0, 0:256], WY.rearrange("p c i -> p (c i)"), ADD).then_inc(S["ws_out"], 1)
            dve.wait_ge(S["u_ps"], NC)
            tell("u_out", v.tensor_copy(Usb.rearrange("p c i -> p (c i)"), ps[:, 1, 0:256]))
            for c in range(CT):
                last = tt(Um[:, c, :, :], Usb[:, c, :].unsqueeze(1).broadcast_to([P, NB, CH]), own, MUL)
            tell("um_ready", last, False)
            for c in range(CT):
                last = tt(Vm[:, c, :, :], Vtok[:, NC - 1, c, :].unsqueeze(1).broadcast_to([P, NB, CH]), own, MUL)
            tell("um_ready", last, False)
            dve.wait_ge(S["ys_ps"], NC)
            ysam = yT[:, :, SEQ:TOK]
            link(v.tensor_copy(ysam, ps[:, 2, 0:128].rearrange("p (c t) -> p c t", c=CT)))
            tell("y_out", tt(ysam, ysam, ps[:, 3, 0:128].rearrange("p (c t) -> p c t", c=CT), ADD))
            rsb = rs[:, :].unsqueeze(1).broadcast_to([P, CT, TOK])
            cv = mix[:, CT:, :]
            dve.wait_ge(S["sum_ps"], 5)
            link(v.tensor_scalar(rs[:, :], ps[:, 1, 0:TOK], 1.0 / (CT * P), None, MUL))
            tell("cc", tt(cv, cv, rsb, SUB))
            dve.wait_ge(S["sd_ps"], 1)
            S0f = S0s.rearrange("p c b i -> p c (b i)")
            tell("snew", tt(S0f, S0f, ps[:, 4:8, :], ADD), False)
            dve.wait_ge(S["root"], 4)
            link(tt(cv, cv, rsb, MUL))
            for c in range(CT):
                tell("cnorm", v.tensor_scalar(cv[:, c, :], cv[:, c, :], V("cln_g", c), V("cln_b", c), MUL, ADD), c == CT - 1)
            y0 = yT[:, :, 0:TOK]
            dve.wait_ge(S["sum_ps"], 7)
            tell("yc", tt(y0, y0, ps[:, 0:4, 0:TOK], SUB))
            dve.wait_ge(S["csig"], 1)
            tell("mix_done", tt(cv, cv, t1[:, :, 0:TOK], MUL), False)
            dve.wait_ge(S["snew"], 1)
            S0c = S0s.rearrange("p c b i -> p (c b) i")
            tell("snew", tt(S0c, S0c, PCs[:, :, :].rearrange("p c b -> p (c b)").unsqueeze(2).broadcast_to([P, CT * NB, CH]), MUL), False)
            dve.wait_ge(S["root"], 5)
            link(tt(y0, y0, t2[:, :, 0:TOK], MUL))
            for c in range(CT):
                last = v.tensor_scalar(y0[:, c, :], y0[:, c, :], V("gn_g", c), V("gn_b", c), MUL, ADD)
            link(last)
            link(tt(y0, y0, mix[:, 0:CT, :], ADD))
            tell("mix_done", tt(mix[:, 0:CT, :], y0, gate[:, :, 0:TOK], MUL))
            for m in range(KT):
                dve.wait_ge(S["wout_ps"], m + 1)
                tell("xres", tt(xT[:, m, 0:TOK], xT[:, m, 0:TOK], ps[:, m, 0:TOK], ADD))
            norm(6, xT, hT, rs[:, :], TOK, "g_x", "h_done")
            dve.wait_ge(S["router_in"], 32)
            tell("wr_ready", tt(w_r, w_r, g_moe.unsqueeze(2).broadcast_to([P, KT, NE]), MUL), False)
            dve.wait_ge(S["s_ps"], 1)
            link(v.tensor_reduce(amax[:, 0:8], ps[:, 0:4, :].rearrange("p h (t m) -> p (h t) m", t=2), AX.X, ALU.max))
            tell("s_max", v.tensor_scalar(amax[:, 0:8], amax[:, 0:8], -1.0 / 16, None, MUL))
            dve.wait_ge(S["s_exp"], 8)
            link(v.reciprocal(asum[:, 0:8], asum[:, 0:8]))
            tell("s_norm", tt(probs, probs, asum[:, 0:8].unsqueeze(2).broadcast_to([P, 8, MEM]), MUL))
            dve.wait_ge(S["sk_ps"], 4)
            dve.wait_ge(S["conv_sent"], 16 * 9)
            link(tt(ssam, ps[:, 4:8, :].rearrange("p n (b m) -> p (n b) m", b=2),
                              C("not_sample").unsqueeze(2).broadcast_to([P, NB, MEM]), ADD))
            flat_s = ssam.rearrange("p b m -> p (b m)")
            link(v.tensor_reduce(amax[:, 8:9], flat_s, AX.X, ALU.max))
            tell("ss_max", v.tensor_scalar(amax[:, 8:9], amax[:, 8:9], -1.0 / 16, None, MUL))
            dve.wait_ge(S["ss_exp"], 1)
            link(v.reciprocal(asum[:, 8:9], asum[:, 8:9]))
            tell("ss_norm", v.tensor_scalar(flat_s, flat_s, asum[:, 8:9], None, MUL))
            for m in range(KT):
                dve.wait_ge(S["wo_ps"], m + 1)
                tell("xres2", tt(xT[:, m, 0:TOK], xT[:, m, 0:TOK], ps[:, m % 6, 0:TOK], ADD), False)
            link = Chain(dve, S["dve_m"])
            dve.wait_ge(S["root"], 7)
            dve.wait_ge(S["logit_ps"], 1)
            for j in range(TT):
                nc.vector.scalar_tensor_tensor(logit[:, j, :], psT[:, j * NE:(j + 1) * NE], rstd[:, j:j + 1], b_r,
                                               ALU.mult, ALU.add).then_inc(S["dve_m"], 1)
            link.n += 3
            dve.wait_ge(S["dve_m"], link.n)
            for j in range(TT):
                nc.vector.max(top8[:, j, :], logit[:, j, :]).then_inc(S["dve_m"], 1)
            link.n += 3
            dve.wait_ge(S["dve_m"], link.n)
            nc.vector.tensor_scalar(ntop, top8[:, :, 0], -1.0, None, ALU.mult).then_inc(S["max_done"], 1)
            v4 = top8[:, :, 3].unsqueeze(2).broadcast_to([P, TT, NE])
            nc.vector.tensor_tensor(over[:, :, :], logit[:, :, :], v4, ALU.is_gt).then_inc(S["dve_m"], 1)
            nc.vector.tensor_tensor(tie[:, :, :], logit[:, :, :], v4, ALU.is_equal).then_inc(S["dve_m"], 1)
            link.n += 2
            dve.wait_ge(S["dve_m"], link.n)
            nc.vector.tensor_reduce(need, over[:, :, :], AX.X, ALU.add).then_inc(S["dve_m"], 1)
            dve.wait_ge(S["pool_c"], 1)
            for j in range(TT):
                nc.vector.tensor_tensor_scan(tiecum[:, j, :], zero, tie[:, j, :], 0.0, ALU.mult, ALU.add).then_inc(S["dve_m"], 1)
            link.n += 4
            dve.wait_ge(S["dve_m"], link.n)
            link(nc.vector.tensor_scalar(need, need, -1.0, 4.0, ALU.mult, ALU.add))
            for j in range(TT):
                link(nc.vector.scalar_tensor_tensor(tie[:, j, :], tiecum[:, j, :], need[:, j:j + 1], tie[:, j, :], ALU.is_le, ALU.mult))
            link(nc.vector.tensor_tensor(mask[:, :, :], over[:, :, :], tie[:, :, :], ALU.add))
            nc.vector.tensor_tensor(mask[:, :, :], mask[:, :, :], valid.unsqueeze(2).broadcast_to([P, TT, NE]), ALU.mult).then_inc(S["mask_done"], 1)
            dve.wait_ge(S["mask_done"], 1)
            dve.wait_ge(S["exp_done"], 3)
            link(nc.vector.tensor_tensor(comb[:, :, 0:NE], comb[:, :, 0:NE], mask[:, :, :], ALU.mult))
            link(nc.vector.tensor_reduce(esum, comb[:, :, 0:NE], AX.X, ALU.add))
            link(nc.vector.tensor_scalar(esum, esum, 1e-30, None, ALU.max))
            link(nc.vector.reciprocal(esum, esum))
            link(nc.vector.tensor_tensor(comb[:, :, 0:NE], comb[:, :, 0:NE], esum.unsqueeze(2).broadcast_to([P, TT, NE]), ALU.mult))
            dve.wait_ge(S["pos_ps"], 1)
            link(nc.vector.scalar_tensor_tensor(pos[:, :, 0:NE], psG[:, 0:TT * NE].rearrange("p (j e) -> p j e", e=NE), 1.0,
                                           mask[:, :, :], ALU.add, ALU.mult))
            nc.vector.tensor_scalar(pos[:, :, 0:NE], pos[:, :, 0:NE], CAP - 1.0, None, ALU.add).then_inc(S["dve_m"], 1)
            nc.vector.tensor_reduce(load, psG[:, TT * NE:(TT + 1) * NE], AX.X, ALU.max).then_inc(S["dve_m"], 1)
            link.n += 2
            dve.wait_ge(S["dve_m"], link.n)
            nc.vector.tensor_copy(load_i[:, :], load).then_inc(S["route_ready"], 1)
            dve.wait_ge(S["route_ready"], 1)
            n = dve.value_load(load_i[0:1, 0:1], min_val=0, max_val=TOK)
            base = link.n

            PICKS, LINKS = 2, 4
            per_round = (PAIRS + 1) * PICKS + PAIRS * LINKS

            def make_pick(q, link):
                for p in range(2):
                    nc.vector.tensor_tensor(pick[:, :, p, :], iota[:, 0:CAP].unsqueeze(1).broadcast_to([P, TT, CAP]),
                                            pos[:, :, bass.ds(2 * q + p, 1)].broadcast_to([P, TT, CAP]), ALU.is_equal).then_inc(S["dve_m"], 1)
                link.n += 2
                dve.wait_ge(S["dve_m"], link.base + link.n)
                for p in range(2):
                    for h in range(2):
                        last = nc.vector.tensor_tensor(wpick[:, :, h, h ^ p, :], pick[:, :, p, :],
                                                       comb[:, :, bass.ds(2 * q + p, 1)].broadcast_to([P, TT, CAP]), ALU.mult)
                last.then_inc(S["pick_ready"], 1)

            def next_round(r):
                nc.vector.tensor_scalar(pos[:, :, 0:NE], pos[:, :, 0:NE], -float(CAP), None, ALU.add).then_inc(S["round_pos"], 1)
                dve.wait_ge(S["round_pos"], r + 1)
                make_pick(0, Chain(dve, S["dve_m"], base + r * per_round))

            def step(r, q, s):
                link = Chain(dve, S["dve_m"], base + r * per_round + PICKS + q * (PICKS + LINKS))
                for p in range(2):
                    last = nc.vector.tensor_copy(one_e[:, p, :], ident[0:NE, bass.ds(2 * q + p, 1)].broadcast_to([NE, CAP]))
                last.then_inc(S["one_ready"], 1)
                dve.wait_ge(S["disp_done"], s + 1)
                nc.vector.tensor_tensor(xe.rearrange("p k a c -> p k (a c)"), psX.rearrange("p (k t) -> p k t", k=KT),
                                        g_moe.unsqueeze(2).broadcast_to([P, KT, 2 * CAP]), ALU.mult).then_inc(S["xe_ready"], 1)

                def gate(p):
                    dve.wait_ge(S["gate_done"], 2 * s + p + 1)
                    nc.vector.tensor_scalar(gmin, psG, 7.0, None, ALU.min).then_inc(S["g_ready"], 1)

                def swiglu(p):
                    dve.wait_ge(S["g_ready"], 2 * s + p + 1)
                    dve.wait_ge(S["up_done"], 2 * s + p + 1)
                    link(nc.vector.tensor_scalar(ug, psU, 7.0, -7.0, ALU.min, ALU.max))
                    link(nc.vector.scalar_tensor_tensor(ug, ug, 1.0, gmin, ALU.add, ALU.mult))
                    dve.wait_ge(S["sig_ready"], 2 * s + p + 1)
                    nc.vector.tensor_tensor(hid, ug, sig, ALU.mult).then_inc(S["hid_ready"], 1)

                gate(0)
                swiglu(0)
                gate(1)
                dve.wait_ge(S["wpickT_done"], s + 1)
                make_pick(q + 1, link)
                swiglu(1)
                for j in range(TT):
                    dve.wait_ge(S["scat_done"], 3 * s + j + 1)
                    nc.vector.tensor_tensor(y[:, j, :], y[:, j, :], psP[(j + 1) % 2][:, :], ALU.add).then_inc(S["y_added"], 1)

            rounds(dve, n, step, next_round)
            nc.vector.tensor_copy(load, load_i[:, :]).then_inc(S["fin_ssq"], 1)
            dve.wait_ge(S["root"], 8)
            for j in range(TT):
                nc.vector.scalar_tensor_tensor(h_tok[:, j, :], y[:, j, :], rstd[:, j:j + 1], gf_row, ALU.mult, ALU.mult).then_inc(S["out_ready"], 1)


def constants():
    import numpy as np
    c = np.zeros((P, CONSTW), np.float32)

    def put(name, a):
        at, n = CONST[name]
        c[:, at:at + n] = a

    p = np.arange(P)[:, None]
    t = np.arange(P)[None, :]
    put("ident", p == t)
    put("ones", 1)
    put("before", p < t)
    put("mean64", (p // CH == t // CH) / CH)
    put("iota", np.arange(CAP)[None, :])
    put("istack", p % CH == np.arange(CH)[None, :])
    s = p % CH
    u = t % CH
    causal = np.where(t < CH, s < u, s <= u)
    put("causal", causal)
    put("causal_s", causal & (s // NT == u // NT) & (s < NB * NT) & (u < NB * NT))
    u = np.arange(CH)[None, :]
    put("levels", np.concatenate([(s // (2 * b) == u // (2 * b)) & (s // b < u // b) for b in (1,) + LEVELS], axis=1))
    put("of_sample", p % (NB * NT) // NT == np.arange(NB)[None, :])
    put("not_sample", np.where(p % (NB * NT) // NT == np.arange(NB)[None, :], 0, -1e30))
    put("valid", np.arange(TT)[None, :] * P + p < TOK)
    return c


def kernel(**inputs):
    import numpy as np
    import concourse.bacc as bacc
    from concourse.bass_utils import run_bass_kernel_spmd as run
    a = {k: np.asarray(v) for k, v in inputs.items()}
    f = np.float32

    def cols(v):
        return v.reshape(-1, P).T

    def halves(w):
        return np.stack([w[:, n * 512:(n + 1) * 512].reshape(KT, P, 512).transpose(1, 0, 2).reshape(P, -1) for n in range(2)])

    xT = np.zeros((P, KT, TT * P), f)
    xT[:, :, 0:TOK] = np.concatenate([a["x_prompt"][0], a["x_sample"].reshape(-1, D)]).T.reshape(KT, P, TOK).transpose(1, 0, 2)
    w_in = a["w_in"][0].reshape(KT, P, -1, P)
    w_in = w_in[:, :, list(W_IN_ORDER), :]
    fills = [w_in[:, :, 4 * n:4 * n + 4, :].transpose(1, 0, 2, 3).reshape(P, -1) for n in range(6)]
    vec = np.concatenate([cols(a[n][0]) for n in ("g_mix", "g_mem", "g_xattn", "g_moe", "mu_shift", "w0", "a0", "k_k", "k_a")]
                         + [cols(a["r_k"].reshape(-1))] + [cols(a[n][0]) for n in ("gn_g", "gn_b", "dw_b", "cln_g", "cln_b")]
                         + [a["dw_w"][0].reshape(TAPS, CT, P).transpose(2, 1, 0).reshape(P, -1)], axis=1)
    arr = {
        "xT": xT, "const": constants(), "vec": vec,
        "memT": a["mem_prompt"][0].T.reshape(KT, P, MEM).transpose(1, 0, 2),
        "lora_wa": np.concatenate([a["w_decay_up"][0], a["w_iclr_up"][0]]), "lora_g": a["w_glora_up"][0],
        "shift": a["state_shift"][0].reshape(NB, RW, P).transpose(2, 1, 0),
        "conv": a["state_conv"][0].reshape(NB, TAPS - 1, CT, P).transpose(3, 2, 0, 1),
        "states": a["state_wkv"][0].reshape(NB, CT, 2, CH, CH).transpose(2, 4, 1, 0, 3).reshape(P, CT, NB, CH),
        "w_mk": halves(a["w_mk"][0]), "w_mv": halves(a["w_mv"][0]), "w_out": halves(a["w_out"][0]),
        "w_q": halves(a["w_q"][0]), "w_o": halves(a["w_o"][0]),
        "cache_k": a["cache_mem_k"][0].reshape(4, 2, MEM, KT, P).transpose(0, 4, 1, 3, 2).reshape(4, P, -1),
        "cache_v": a["cache_mem_v"][0].reshape(4, 2, 2, P, D).transpose(0, 3, 1, 2, 4).reshape(4, P, -1),
        "g_final_row": a["g_final"].reshape(1, D),
        "w_router": a["w_router"][0].reshape(KT, P, NE).transpose(1, 0, 2), "b_router": a["b_router"],
        "b_gate": a["b_moe_gate"][0], "b_up": a["b_moe_up"][0], "b_down": a["b_moe_down"][0],
        "w_gate": a["w_moe_gate"][0], "w_up": a["w_moe_up"][0], "w_down": a["w_moe_down"][0],
    }
    for n in range(6):
        arr[f"w_in{n}"] = fills[n]
    nc = bacc.Bacc("TRN2", target_bir_lowering=False, num_devices=1)
    A, feed = {}, {}
    for k, v in arr.items():
        v = np.ascontiguousarray(v)
        feed["in_" + k] = v
        A[k] = nc.dram_tensor("in_" + k, v.shape, F32, kind="ExternalInput").ap()
    A["w_in"] = [A[f"w_in{n}"] for n in range(6)]
    O = {k: nc.dram_tensor("out_" + k, s, F32, kind="ExternalOutput").ap() for k, s in dict(
        y=(P, TT, D), shift=(P, RW, 1 + NB), conv=(P, CT, 1 + NB, TAPS - 1), state_p=(P, CT, CH),
        state_s=(P, CT, NB, CH), mem_k=(P, KT, MEM), mem_v=(P, 2, D)).items()}
    build(nc, A, O)
    r = run(nc, [feed], core_ids=[0]).results[0]
    y = r["out_y"].transpose(1, 0, 2).reshape(TT * P, D)
    shift = r["out_shift"].transpose(2, 1, 0).reshape(1 + NB, RW * P)
    conv = r["out_conv"].transpose(2, 3, 1, 0).reshape(1 + NB, TAPS - 1, CT * P)
    sp = r["out_state_p"].reshape(2, CH, CT, CH).transpose(2, 0, 3, 1).reshape(1, 2 * CT, CH, CH)
    ss = r["out_state_s"].reshape(2, CH, CT, NB, CH).transpose(3, 2, 0, 4, 1).reshape(NB, 2 * CT, CH, CH)
    mk = r["out_mem_k"].transpose(2, 1, 0).reshape(1, MEM, XH, D // XH)
    mv = r["out_mem_v"].transpose(1, 0, 2).reshape(1, MEM, XH, D // XH)
    return (y[0:SEQ].reshape(1, SEQ, D), y[SEQ:TOK].reshape(NB, NT, D), shift[None, 0:1], sp[None], conv[None, 0:1],
            mk[None], mv[None], shift[None, 1:], ss[None], conv[None, 1:])
```
